# Optimizing a Trainium2 kernel written in Bass

```python
import jax, jax.numpy as jnp
from jax import lax
import numpy as np

D_MODEL = 1024
BATCH = 1
SEQ = 4096
DEPTH = 2

N_A_LAYERS = DEPTH // 2
N_B_LAYERS = DEPTH - N_A_LAYERS
POOL_WINDOWS = (2, 4, 8, 16)
N_POOL_GROUPS = len(POOL_WINDOWS)
POOL_GROUP = D_MODEL // N_POOL_GROUPS
MAX_POOL = max(POOL_WINDOWS)
HEAD_DIM = 64
N_Q_HEADS = D_MODEL // HEAD_DIM
N_KV_HEADS = 4
Q_PER_KV = N_Q_HEADS // N_KV_HEADS
WINDOW = 128
BLOCK = 128
ROPE_THETA = 10000.0
N_GROUPS = 4
EXPERTS_PER_GROUP = 8
N_EXPERTS = N_GROUPS * EXPERTS_PER_GROUP
TOP_K_IN_GROUP = 2
D_EXPERT = 512
PLE_DIM = 256
EPS = 1e-6

kernel_name = 'yoco_pool_swa_sink_hier_moe_ple'

def rmsnorm(x, g):
    xf = x.astype(jnp.float32)
    y = xf * lax.rsqrt(jnp.mean(xf * xf, axis=-1, keepdims=True) + EPS)
    return (y * g.astype(jnp.float32)).astype(x.dtype)

def rope_tables(positions):
    inv = ROPE_THETA ** (-jnp.arange(0, HEAD_DIM, 2, dtype=jnp.float32) / HEAD_DIM)
    ang = positions.astype(jnp.float32)[..., None] * inv
    return jnp.cos(ang)[:, :, None, :], jnp.sin(ang)[:, :, None, :]

def apply_rope(x, cos, sin):
    xf = x.astype(jnp.float32)
    x1, x2 = jnp.split(xf, 2, axis=-1)
    out = jnp.concatenate([x1 * cos - x2 * sin, x2 * cos + x1 * sin], axis=-1)
    return out.astype(x.dtype)

def pool_mixer(hn, w_pool, scale):
    B, S, D = hn.shape
    xg = hn.reshape(B, S, N_POOL_GROUPS, POOL_GROUP).astype(jnp.float32)
    c = jnp.cumsum(xg, axis=1)
    c = jnp.pad(c, ((0, 0), (MAX_POOL, 0), (0, 0), (0, 0)))
    t = jnp.arange(S)
    means = []
    for gi, w in enumerate(POOL_WINDOWS):
        win_sum = c[:, MAX_POOL:, gi] - c[:, MAX_POOL - w:MAX_POOL - w + S, gi]
        cnt = jnp.minimum(t + 1, w).astype(jnp.float32)
        means.append(win_sum / cnt[None, :, None])
    d = (jnp.stack(means, axis=2) - xg).astype(hn.dtype)
    y = jnp.einsum('bsgc,gce->bsge', d, w_pool).reshape(B, S, D)
    return y * scale

def shared_kv(h, g_kv, w_k, w_v, cos, sin):
    B, S, _ = h.shape
    hn = rmsnorm(h, g_kv)
    k = apply_rope((hn @ w_k).reshape(B, S, N_KV_HEADS, HEAD_DIM), cos, sin)
    v = (hn @ w_v).reshape(B, S, N_KV_HEADS, HEAD_DIM)
    return k, v

def banded_blocks(t, nb):
    B = t.shape[0]
    tp = jnp.pad(t, ((0, 0), (BLOCK, 0), (0, 0), (0, 0)))
    tb = tp.reshape(B, nb + 1, BLOCK, N_KV_HEADS, HEAD_DIM)
    return jnp.concatenate([tb[:, :-1], tb[:, 1:]], axis=2)

def swa_sink_attention(hn, w_q, w_o, sinks, k, v, cos, sin):
    B, S, D = hn.shape
    nb = S // BLOCK
    q = apply_rope((hn @ w_q).reshape(B, S, N_Q_HEADS, HEAD_DIM), cos, sin)
    q = (q * (HEAD_DIM ** -0.5)).reshape(B, nb, BLOCK, N_KV_HEADS, Q_PER_KV, HEAD_DIM)
    kb = banded_blocks(k, nb)
    vb = banded_blocks(v, nb)
    s = jnp.einsum('bnqkgd,bnjkd->bnkgqj', q, kb).astype(jnp.float32)
    i = jnp.arange(BLOCK)[:, None]
    j = jnp.arange(2 * BLOCK)[None, :]
    rel = i + BLOCK - j
    band = (rel >= 0) & (rel < WINDOW)
    valid = (jnp.arange(nb)[:, None, None] > 0) | (j >= BLOCK)[None]
    mask = (band[None] & valid)[None, :, None, None]
    s = jnp.where(mask, s, -jnp.inf)
    sink = sinks.astype(jnp.float32).reshape(1, 1, N_KV_HEADS, Q_PER_KV, 1, 1)
    m = jnp.maximum(jnp.max(s, axis=-1, keepdims=True), sink)
    e = jnp.exp(s - m)
    pr = (e / (jnp.sum(e, axis=-1, keepdims=True) + jnp.exp(sink - m))).astype(vb.dtype)
    o = jnp.einsum('bnkgqj,bnjkd->bnqkgd', pr, vb).reshape(B, S, N_Q_HEADS * HEAD_DIM)
    return o @ w_o

def hierarchical_moe(hn, w_grp, b_grp, w_exp_r, b_exp_r, w_gate, w_up, w_down):
    B, S, D = hn.shape
    T = B * S
    xt = hn.reshape(T, D)
    gl = (xt @ w_grp).astype(jnp.float32) + b_grp.astype(jnp.float32)
    gp = jax.nn.softmax(gl, axis=-1)
    pg, gsel = lax.top_k(gp, 1)
    el = ((xt @ w_exp_r).astype(jnp.float32) + b_exp_r.astype(jnp.float32))
    el = el.reshape(T, N_GROUPS, EXPERTS_PER_GROUP)
    el_sel = jnp.take_along_axis(el, gsel[:, :, None], axis=1)[:, 0]
    top_logit, eidx = lax.top_k(el_sel, TOP_K_IN_GROUP)
    gates = pg * jax.nn.softmax(top_logit, axis=-1)
    expert_id = gsel * EXPERTS_PER_GROUP + eidx
    flat_e = expert_id.reshape(-1)
    flat_tok = jnp.repeat(jnp.arange(T, dtype=jnp.int32), TOP_K_IN_GROUP)
    flat_g = gates.reshape(-1)
    order = jnp.argsort(flat_e)
    stok = flat_tok[order]
    sg = flat_g[order]
    group_sizes = jnp.bincount(flat_e, length=N_EXPERTS).astype(jnp.int32)
    xs = xt[stok]
    a = jax.nn.silu(lax.ragged_dot(xs, w_gate, group_sizes)) * lax.ragged_dot(xs, w_up, group_sizes)
    y = lax.ragged_dot(a, w_down, group_sizes) * sg[:, None].astype(xs.dtype)
    out = jnp.zeros((T, D), y.dtype).at[stok].add(y)
    return out.reshape(B, S, D).astype(hn.dtype)

def per_layer_embedding(h, p_i, g_ple, w_ple_gate, w_ple_up):
    gate = jax.nn.sigmoid(rmsnorm(h, g_ple) @ w_ple_gate)
    return h + gate * (p_i @ w_ple_up)

def setup_inputs(seed: int = 0) -> dict:
    key = jax.random.key(seed)
    ks = jax.random.split(key, 32)
    f32 = jnp.float32

    def nrm(k, shape, scale):
        return jax.random.normal(k, shape, f32) * scale

    D = D_MODEL
    QD = N_Q_HEADS * HEAD_DIM
    KD = N_KV_HEADS * HEAD_DIM
    positions = (jnp.arange(SEQ, dtype=jnp.int32)[None, :]
                 + jax.random.randint(ks[2], (BATCH, 1), 0, 1024, dtype=jnp.int32))
    return {
        'x': nrm(ks[0], (BATCH, SEQ, D), 1.0),
        'p': nrm(ks[1], (DEPTH, BATCH, SEQ, PLE_DIM), 1.0),
        'positions': positions,
        'g_mix': 1.0 + nrm(ks[3], (DEPTH, D), 0.05),
        'g_ffn': 1.0 + nrm(ks[4], (DEPTH, D), 0.05),
        'pool_w': nrm(ks[5], (N_A_LAYERS, N_POOL_GROUPS, POOL_GROUP, POOL_GROUP), POOL_GROUP ** -0.5),
        'pool_scale': 1.0 + nrm(ks[6], (N_A_LAYERS, D), 0.1),
        'g_kv': 1.0 + nrm(ks[7], (D,), 0.05),
        'w_k': nrm(ks[8], (D, KD), D ** -0.5),
        'w_v': nrm(ks[9], (D, KD), D ** -0.5),
        'w_q': nrm(ks[10], (N_B_LAYERS, D, QD), D ** -0.5),
        'w_o': nrm(ks[11], (N_B_LAYERS, QD, D), QD ** -0.5),
        'sinks': nrm(ks[12], (N_B_LAYERS, N_Q_HEADS), 0.5),
        'w_group_router': nrm(ks[13], (DEPTH, D, N_GROUPS), D ** -0.5),
        'b_group_router': nrm(ks[14], (DEPTH, N_GROUPS), 0.01),
        'w_expert_router': nrm(ks[15], (DEPTH, D, N_EXPERTS), D ** -0.5),
        'b_expert_router': nrm(ks[16], (DEPTH, N_EXPERTS), 0.01),
        'w_exp_gate': nrm(ks[17], (DEPTH, N_EXPERTS, D, D_EXPERT), D ** -0.5),
        'w_exp_up': nrm(ks[18], (DEPTH, N_EXPERTS, D, D_EXPERT), D ** -0.5),
        'w_exp_down': nrm(ks[19], (DEPTH, N_EXPERTS, D_EXPERT, D), D_EXPERT ** -0.5),
        'g_ple': 1.0 + nrm(ks[20], (DEPTH, D), 0.05),
        'w_ple_gate': nrm(ks[21], (DEPTH, D, D), D ** -0.5),
        'w_ple_up': nrm(ks[22], (DEPTH, PLE_DIM, D), 0.5 * PLE_DIM ** -0.5),
        'g_final': 1.0 + nrm(ks[23], (D,), 0.05),
    }

def reference(x, p, positions, g_mix, g_ffn, pool_w, pool_scale, g_kv, w_k, w_v, w_q, w_o, sinks,
              w_group_router, b_group_router, w_expert_router, b_expert_router,
              w_exp_gate, w_exp_up, w_exp_down, g_ple, w_ple_gate, w_ple_up, g_final):
    cos, sin = rope_tables(positions)
    h = x
    k_sh = None
    v_sh = None
    for i in range(DEPTH):
        hn = rmsnorm(h, g_mix[i])
        if i < N_A_LAYERS:
            h = h + pool_mixer(hn, pool_w[i], pool_scale[i])
        else:
            jb = i - N_A_LAYERS
            h = h + swa_sink_attention(hn, w_q[jb], w_o[jb], sinks[jb], k_sh, v_sh, cos, sin)
        h = h + hierarchical_moe(rmsnorm(h, g_ffn[i]), w_group_router[i], b_group_router[i],
                                 w_expert_router[i], b_expert_router[i],
                                 w_exp_gate[i], w_exp_up[i], w_exp_down[i])
        h = per_layer_embedding(h, p[i], g_ple[i], w_ple_gate[i], w_ple_up[i])
        if i == N_A_LAYERS - 1:
            k_sh, v_sh = shared_kv(h, g_kv, w_k, w_v, cos, sin)
    return rmsnorm(h, g_final)


_drawn_inputs = setup_inputs


def setup_inputs(seed=0):
    import zlib

    import numpy as np

    out = dict(_drawn_inputs(seed))
    spreads = {}
    factors = {'g_kv': 4.008,
     'sinks': 24.594,
     'b_group_router': 3.15,
     'b_expert_router': 2.951,
     'g_ple': 5.188}
    for name, (base, spread) in spreads.items():
        noise = np.random.default_rng([zlib.crc32(name.encode()), seed]).standard_normal(out[name].shape)
        drawn = base * np.exp(spread * noise) if base else spread * noise
        out[name] = __import__('jax').numpy.asarray(drawn.astype(out[name].dtype))
    for name, factor in factors.items():
        out[name] = (out[name] * factor).astype(out[name].dtype)
    return out
```

```python
from contextlib import ExitStack

import numpy as np

import concourse.bass as bass
from concourse import mybir

F32 = mybir.dt.float32
BF16 = mybir.dt.bfloat16
I32 = mybir.dt.int32
U32 = mybir.dt.uint32
ALU = mybir.AluOpType
ACT = mybir.ActivationFunctionType
AX_X = mybir.AxisListType.X

P = 128
D = 1024
T = 4096
NT = T // P
KD = D // P
WINDOWS = (2, 4, 8, 16)
POOL_GROUP = D // len(WINDOWS)
TAIL = max(WINDOWS)
HEAD = 64
NQ = 16
NKV = 4
KVW = NKV * HEAD
NGRP = 4
EPG = 8
NE = NGRP * EPG
NLOG = NGRP + NE
F = 512
KF = F // P
PLE = 256
KPLE = PLE // P
EPS = 1e-6
NEG = -1.0e30
MAX_TILES = 2 * NT + NE
WCHUNK = 2048
NCHUNK = 3 * D * F // P // WCHUNK
POOL_CHUNKS = 3
INV_FREQ = (np.float32(10000.0) ** (-np.arange(0, HEAD, 2, dtype=np.float32) / np.float32(HEAD))).astype(np.float32)


def wait(eng, sem, value):
    if isinstance(value, int) and value <= 0:
        return
    eng.wait_ge(sem, value)


class Mem:

    def __init__(self, nc, tag, stack):
        self.nc, self.tag, self.stack = nc, tag, stack
        stack.enter_context(nc.cleanup_on_exit())

    def sb(self, name, shape, dt=F32):
        return self.stack.enter_context(self.nc.sbuf_tensor(f"{self.tag}_{name}", shape, dt))

    def ps(self, name, shape, dt=F32):
        return self.stack.enter_context(self.nc.psum_tensor(f"{self.tag}_ps_{name}", shape, dt))

    def sem(self, name):
        return self.nc.alloc_semaphore(f"{self.tag}_{name}")

    def sems(self, names):
        return [self.sem(n) for n in names.split()]


def row(vec):
    n = vec.shape[0]
    return vec.rearrange("(o n) -> o n", o=1).to_broadcast([P, n])


def mm3(pe, out, lhs_hi, lhs_lo, rhs_hi, rhs_lo, first, last):
    pe.matmul(out, lhs_hi, rhs_hi, start=first, stop=False)
    pe.matmul(out, lhs_hi, rhs_lo, start=False, stop=False)
    return pe.matmul(out, lhs_lo, rhs_hi, start=False, stop=last)


def constants_phase(nc, C):
    with ExitStack() as stack:
        m = Mem(nc, "cst", stack)
        keep = m.sb("keep", [P, 4, P])
        count = m.sb("count", [P, P])
        inv_count = m.sb("inv_count", [P, 4, P])
        filled, masked, band_ready = m.sems("filled masked band_ready")
        block = stack.enter_context(nc.Block())

        @block.gpsimd
        def _(pool):
            pool.memset(C.ident[:], 0.0).then_inc(filled, 1)
            pool.memset(C.before[:], 1.0).then_inc(filled, 1)
            pool.memset(C.ones[:], 1.0).then_inc(filled, 1)
            pool.memset(keep[:], 1.0).then_inc(filled, 1)
            for g, w in enumerate(WINDOWS):
                pool.memset(C.band_prev[:, g, :], 1.0 / w).then_inc(filled, 1)
            pool.memset(C.minus_half[:], -0.5).then_inc(filled, 1)
            pool.memset(C.mask_first[:, 0:P], NEG).then_inc(filled, 1)
            pool.memset(C.mask_first[:, P:2 * P], 0.0).then_inc(filled, 1)
            pool.memset(C.mask[:], 0.0).then_inc(filled, 1)
            pool.wait_ge(filled, 12)
            pool.affine_select(out=C.ident[:], in_=C.ident[:], compare_op=ALU.not_equal, fill=1.0, base=0,
                               pattern=[[-1, P]], channel_multiplier=1).then_inc(masked, 1)
            pool.affine_select(out=C.before[:], in_=C.before[:], compare_op=ALU.is_ge, fill=0.0, base=-1,
                               pattern=[[1, P]], channel_multiplier=-1).then_inc(masked, 1)
            pool.affine_select(out=keep[:], in_=keep[:], compare_op=ALU.is_ge, fill=0.0, base=0,
                               pattern=[[0, 4], [1, P]], channel_multiplier=-1).then_inc(masked, 1)
            pool.affine_select(out=C.mask[:, P:2 * P], in_=C.mask[:, P:2 * P], compare_op=ALU.is_ge, fill=NEG,
                               base=0, pattern=[[-1, P]], channel_multiplier=1).then_inc(masked, 1)
            pool.affine_select(out=C.mask[:, 0:P], in_=C.mask[:, 0:P], compare_op=ALU.is_ge, fill=NEG,
                               base=-1, pattern=[[1, P]], channel_multiplier=-1).then_inc(masked, 1)
            pool.affine_select(out=C.mask_first[:, P:2 * P], in_=C.mask_first[:, P:2 * P], compare_op=ALU.is_ge,
                               fill=NEG, base=0, pattern=[[-1, P]], channel_multiplier=1).then_inc(masked, 1)
            for g, w in enumerate(WINDOWS):
                pool.affine_select(out=C.band_prev[:, g, :], in_=C.band_prev[:, g, :], compare_op=ALU.is_ge,
                                   fill=0.0, base=w - 1 - P, pattern=[[-1, TAIL]],
                                   channel_multiplier=1).then_inc(masked, 1)
            pool.wait_ge(masked, 10)
            for g, w in enumerate(WINDOWS):
                pool.affine_select(out=keep[:, g, :], in_=keep[:, g, :], compare_op=ALU.is_ge, fill=0.0,
                                   base=w - 1, pattern=[[-1, P]], channel_multiplier=1).then_inc(masked, 1)
            pool.iota(count[:], pattern=[[1, P]], base=1, channel_multiplier=0,
                      allow_small_or_imprecise_dtypes=True).then_inc(masked, 1)
            pool.iota(C.iota[:], pattern=[[1, P]], base=0, channel_multiplier=0,
                      allow_small_or_imprecise_dtypes=True).then_inc(masked, 1)
            pool.iota(C.lane[:], pattern=[[0, 1]], base=0, channel_multiplier=1,
                      allow_small_or_imprecise_dtypes=True).then_inc(masked, 1)

        @block.vector
        def _(dve):
            dve.wait_ge(masked, 17)
            dve.tensor_copy(C.ident_bf[:], C.ident[:]).then_inc(band_ready, 1)
            for g, w in enumerate(WINDOWS):
                dve.tensor_scalar(inv_count[:, g, :], count[:], float(w), None, ALU.min).then_inc(band_ready, 1)
            dve.wait_ge(band_ready, 5)
            dve.reciprocal(inv_count[:], inv_count[:]).then_inc(band_ready, 1)
            dve.wait_ge(band_ready, 6)
            dve.tensor_tensor(inv_count[:], inv_count[:], keep[:], ALU.mult).then_inc(band_ready, 1)
            dve.wait_ge(band_ready, 7)
            for g, w in enumerate(WINDOWS):
                dve.scalar_tensor_tensor(out=C.band[:, g, :], in0=keep[:, g, :], scalar=1.0 / w, in1=C.ident[:],
                                         op0=ALU.mult, op1=ALU.subtract).then_inc(band_ready, 1)
                dve.tensor_tensor(C.band_first[:, g, :], inv_count[:, g, :], C.ident[:],
                                  ALU.subtract).then_inc(band_ready, 1)


def load_router(nc, sp, A, m_wr, m_bias, layer, loaded):
    with nc.allow_non_contiguous_dma(reason="router columns, once"):
        sp.dma_start(m_wr[:, :, 0:NGRP],
                     A["w_group_router"][layer].rearrange("(k p) n -> p k n", p=P)).then_inc(loaded, 16)
        sp.dma_start(m_wr[:, :, NGRP:NLOG],
                     A["w_expert_router"][layer].rearrange("(k p) n -> p k n", p=P)).then_inc(loaded, 16)
        sp.dma_start(m_bias[:, 0:NGRP], row(A["b_group_router"][layer])).then_inc(loaded, 16)
        sp.dma_start(m_bias[:, NGRP:NLOG], row(A["b_expert_router"][layer])).then_inc(loaded, 16)


def pool_phase(nc, A, C):
    with ExitStack() as stack:
        m = Mem(nc, "mix", stack)
        wpool = m.sb("wpool", [P, KD, POOL_GROUP])
        scale_row = m.sb("scale_row", [P, D])
        g_ffn = m.sb("g_ffn", [P, D])
        g_mix = m.sb("g_mix", [P, KD])
        w_router = m.sb("w_router", [P, KD, NLOG])
        bias = m.sb("bias", [P, NLOG])
        x = [m.sb(f"x{u}", [P, D]) for u in (0, 1)]
        xn = [m.sb(f"xn{u}", [P, D]) for u in (0, 1)]
        junk = m.sb("junk", [P, D])
        junk_h = m.sb("junk_h", [P, D])
        pooled = m.sb("pooled", [P, KD, P])
        h1 = [m.sb(f"h1_{u}", [P, D]) for u in (0, 1)]
        hn = [m.sb(f"hn{u}", [P, D]) for u in (0, 1)]
        hnT = m.sb("hnT", [P, KD, P])
        hrow = [m.sb(f"hrow{u}", [P, 2 * D], BF16) for u in (0, 1)]
        ssx, msx, rsx = (m.sb(n, [P, 2]) for n in ("ssx", "msx", "rsx"))
        ssh, msh, rsh = (m.sb(n, [P, 2]) for n in ("ssh", "msh", "rsh"))
        ps_pool = m.ps("pool", [P, KD, P])
        ps_mix = m.ps("mix", [P, D])
        ps_T = m.ps("T", [P, KD, P])
        ps_log = m.ps("log", [P, 512])
        loaded, folded, w_ready = m.sems("loaded folded w_ready")
        x_loaded, h1_stored, row_stored = ([m.sem(f"{n}{u}") for u in (0, 1)] for n in ("x_ld", "h1_st", "row_st"))
        ssx_done, msx_done, rsx_done, xn_done, pool_done, pooled_done, mix_done, h1_done = m.sems(
            "ssx_done msx_done rsx_done xn_done pool_done pooled_done mix_done h1_done")
        ssh_done, msh_done, rsh_done, hn_done, hi_done, lo_done, T_done, hnT_done, log_done, logits_done = m.sems(
            "ssh_done msh_done rsh_done hn_done hi_done lo_done T_done hnT_done log_done logits_done")
        x_t = A["x"].rearrange("b (t p) d -> (b t) p d", p=P)
        h1_t = C.h_mid.rearrange("(t p) d -> t p d", p=P)
        row_t = C.hn_rows.rearrange("(t p) d -> t p d", p=P)
        spare_t = C.y_rows.rearrange("(t p) d -> t p d", p=P)
        zeros = m.sb("zeros", [P, D])
        zeros_done, spare_filled = m.sems("zeros_done spare_filled")
        block = stack.enter_context(nc.Block())

        def steps(eng, step):
            step(0, 0, True, False)
            step(1, 1, True, True)
            with eng.Fori(1, NT // 2) as i:
                step(2 * i, 0, True, True)
                step(2 * i + 1, 1, True, True)
            step(NT, 0, False, True)

        @block.sync
        def _(sp):
            sp.dma_start(x[0][:], x_t[0]).then_inc(x_loaded[0], 16)
            sp.dma_start(wpool[:], A["pool_w"][0].rearrange("g (k p) e -> p (g k) e", p=P)).then_inc(loaded, 16)
            sp.dma_start(scale_row[:], row(A["pool_scale"][0])).then_inc(loaded, 16)
            sp.dma_start(g_ffn[:], row(A["g_ffn"][0])).then_inc(loaded, 16)
            with nc.allow_non_contiguous_dma(reason="one gain per partition, once"):
                sp.dma_start(g_mix[:], A["g_mix"][0].rearrange("(k p) -> p k", p=P)).then_inc(loaded, 16)
            load_router(nc, sp, A, w_router, bias, 0, loaded)

            def step(t, u, mixer, router, more=True):
                v = 1 - u
                if more:
                    wait(sp, h1_done, t)
                    sp.dma_start(x[v][:], x_t[t + 1]).then_inc(x_loaded[v], 16)
                if router:
                    sp.wait_ge(lo_done, t)
                    sp.dma_start(row_t[t - 1], hrow[v][:]).then_inc(row_stored[v], 16)
                if mixer:
                    sp.wait_ge(h1_done, t + 1)
                    sp.dma_start(h1_t[t], h1[u][:]).then_inc(h1_stored[u], 16)
                    sp.dma_start(spare_t[t + (MAX_TILES + 1 - NT)], zeros[:]).then_inc(spare_filled, 16)

            sp.wait_ge(zeros_done, 1)
            step(0, 0, True, False)
            step(1, 1, True, True)
            with sp.Fori(1, NT // 2 - 1) as i:
                step(2 * i, 0, True, True)
                step(2 * i + 1, 1, True, True)
            step(NT - 2, 0, True, True)
            step(NT - 1, 1, True, True, more=False)
            step(NT, 0, False, True, more=False)
            for u in (0, 1):
                sp.wait_ge(h1_stored[u], 8 * NT)
                sp.wait_ge(row_stored[u], 8 * NT)
            sp.wait_ge(spare_filled, 16 * NT)

        @block.gpsimd
        def _(pool):
            pool.memset(zeros[:], 0.0).then_inc(zeros_done, 1)

            def step(t, u, mixer, router):
                v = 1 - u
                if router:
                    pool.wait_ge(msh_done, t)
                    pool.tensor_tensor(rsh[:, v:v + 1], msh[:, v:v + 1], C.minus_half[:], ALU.pow).then_inc(rsh_done, 1)
                if mixer:
                    pool.wait_ge(msx_done, t + 1)
                    pool.tensor_tensor(rsx[:, u:u + 1], msx[:, u:u + 1], C.minus_half[:], ALU.pow).then_inc(rsx_done, 1)

            steps(pool, step)

        @block.scalar
        def _(act):
            def step(t, u, mixer, router):
                v = 1 - u
                if router:
                    act.wait_ge(h1_done, t)
                    act.activation(junk_h[:], h1[v][:], ACT.Square, accum_out=ssh[:, v:v + 1]).then_inc(ssh_done, 1)
                if mixer:
                    act.wait_ge(x_loaded[u], done(t, u))
                    wait(act, ssx_done, t)
                    act.activation(junk[:], x[u][:], ACT.Square, accum_out=ssx[:, u:u + 1]).then_inc(ssx_done, 1)
                    act.wait_ge(rsx_done, t + 1)
                    wait(act, pool_done, t)
                    act.activation(xn[u][:], x[u][:], ACT.Copy, scale=rsx[:, u:u + 1]).then_inc(xn_done, 1)
                if router:
                    act.wait_ge(hn_done, t)
                    wait(act, row_stored[v], done(t - 3, v) if not isinstance(t, int) or t >= 3 else 0)
                    act.activation(hrow[v][:, 0:D], hn[v][:], ACT.Copy).then_inc(hi_done, 1)
                if mixer:
                    act.wait_ge(pool_done, t + 1)
                    wait(act, mix_done, t)
                    act.activation(pooled[:], ps_pool[:], ACT.Copy).then_inc(pooled_done, 1)

            steps(act, step)

        @block.vector
        def _(dve):
            dve.wait_ge(loaded, 16 * 8)
            for k in range(KD):
                g = k * P // POOL_GROUP
                dve.scalar_tensor_tensor(out=wpool[:, k, :], in0=wpool[:, k, :], scalar=g_mix[:, k:k + 1],
                                         in1=scale_row[:, g * POOL_GROUP:(g + 1) * POOL_GROUP],
                                         op0=ALU.mult, op1=ALU.mult).then_inc(w_ready, 1)

            def step(t, u, mixer, router):
                v = 1 - u
                if router:
                    dve.wait_ge(ssh_done, t)
                    dve.tensor_scalar(msh[:, v:v + 1], ssh[:, v:v + 1], 1.0 / D, EPS, ALU.mult, ALU.add).then_inc(msh_done, 1)
                if mixer:
                    dve.wait_ge(ssx_done, t + 1)
                    dve.tensor_scalar(msx[:, u:u + 1], ssx[:, u:u + 1], 1.0 / D, EPS, ALU.mult, ALU.add).then_inc(msx_done, 1)
                if router:
                    dve.wait_ge(rsh_done, t)
                    wait(dve, T_done, t - 2)
                    dve.scalar_tensor_tensor(out=hn[v][:], in0=h1[v][:], scalar=rsh[:, v:v + 1], in1=g_ffn[:],
                                             op0=ALU.mult, op1=ALU.mult).then_inc(hn_done, 1)
                    dve.wait_ge(hi_done, t)
                    dve.wait_ge(hn_done, t)
                    dve.tensor_tensor(hrow[v][:, D:2 * D], hn[v][:], hrow[v][:, 0:D], ALU.subtract).then_inc(lo_done, 1)
                    dve.wait_ge(T_done, t)
                    wait(dve, log_done, t - 1)
                    dve.tensor_copy(hnT[:], ps_T[:]).then_inc(hnT_done, 1)
                if mixer:
                    dve.wait_ge(mix_done, t + 1)
                    wait(dve, h1_stored[u], done(t - 2, u) if not isinstance(t, int) or t >= 2 else 0)
                    dve.tensor_tensor(h1[u][:], ps_mix[:], x[u][:], ALU.add).then_inc(h1_done, 1)
                if router:
                    dve.wait_ge(log_done, t)
                    dve.tensor_tensor(C.logits[:, bass.ds(t - 1, 1), :].rearrange("p a b -> p (a b)"), ps_log[:, 0:NLOG], bias[:],
                                      ALU.add).then_inc(logits_done, 1)

            steps(dve, step)

        @block.tensor
        def _(pe):
            pe.wait_ge(w_ready, KD)

            def step(t, u, mixer, router):
                v = 1 - u
                if mixer:
                    pe.wait_ge(xn_done, t + 1)
                    wait(pe, pooled_done, t)
                    first = isinstance(t, int) and t == 0
                    for k in range(KD):
                        g = k * P // POOL_GROUP
                        band = C.band_first if first else C.band
                        mm = pe.matmul(ps_pool[:, k, :], xn[u][:, k * P:(k + 1) * P], band[:, g, :],
                                       start=True, stop=first)
                        if not first:
                            mm = pe.matmul(ps_pool[:, k, 0:TAIL], xn[v][:, k * P:(k + 1) * P], C.band_prev[:, g, :],
                                           start=False, stop=True)
                    mm.then_inc(pool_done, 1)
                if router:
                    pe.wait_ge(hn_done, t)
                    wait(pe, hnT_done, t - 1)
                    for k in range(KD):
                        mm = pe.transpose(ps_T[:, k, :], hn[v][:, k * P:(k + 1) * P], C.ident[:])
                    mm.then_inc(T_done, 1)
                if mixer:
                    pe.wait_ge(pooled_done, t + 1)
                    wait(pe, h1_done, t)
                    for k in range(KD):
                        g, kk = divmod(k, POOL_GROUP // P)
                        mm = pe.matmul(ps_mix[:, g * POOL_GROUP:(g + 1) * POOL_GROUP], pooled[:, k, :], wpool[:, k, :],
                                       start=kk == 0, stop=kk == POOL_GROUP // P - 1)
                    mm.then_inc(mix_done, 1)
                if router:
                    pe.wait_ge(hnT_done, t)
                    wait(pe, logits_done, t - 1)
                    for k in range(KD):
                        mm = pe.matmul(ps_log[:, 0:NLOG], hnT[:, k, :], w_router[:, k, :], start=k == 0, stop=k == KD - 1)
                    mm.then_inc(log_done, 1)

            steps(pe, step)


def route_phase(nc, C, layer):
    with ExitStack() as stack:
        m = Mem(nc, f"rt{layer}", stack)
        gl = m.sb("gl", [P, NT, 8])
        gmax = m.sb("gmax", [P, NT, 8])
        gidx = m.sb("gidx", [P, NT, 8], U32)
        gsel = m.sb("gsel", [P, NT])
        pen = m.sb("pen", [P, NT, NGRP])
        ex = m.sb("ex", [P, NT, NGRP])
        esum = m.sb("esum", [P, NT])
        el = m.sb("el", [P, NT, NE])
        emax = m.sb("emax", [P, NT, 8])
        eidx = m.sb("eidx", [P, NT, 8], U32)
        esel = m.sb("esel", [P, 2, NT])
        ediff = m.sb("ediff", [P, NT])
        den = m.sb("den", [P, NT])
        one_hot = [m.sb(f"one_hot{c}", [P, NT, NE]) for c in (0, 1)]
        both = m.sb("both", [P, NT, NE])
        total = m.sb("total", [P, NT, NE])
        scan = [m.sb(f"scan{c}", [P, NT, NE]) for c in (0, 1)]
        tiles_i = m.sb("tiles_i", [P, NE], I32)
        tiles_f = [m.sb(f"tiles_f{c}", [P, NE]) for c in (0, 1, 2)]
        ends_f = m.sb("ends_f", [P, NE + 1])
        slot_f = m.sb("slot_f", [P, 2, NT])
        slot_i = m.sb("slot_i", [P, 2, NT], I32)
        lo_i = m.sb("lo_i", [P, 2 * NT], I32)
        hi_i = m.sb("hi_i", [P, 2 * NT], I32)
        lo_f = m.sb("lo_f", [P, 2 * NT])
        hi_f = m.sb("hi_f", [P, 2 * NT])
        B = 8
        is_lo = [m.sb(f"is_lo{c}", [P, B, P], BF16) for c in (0, 1)]
        is_hi = [m.sb(f"is_hi{c}", [P, B, MAX_TILES], BF16) for c in (0, 1)]
        token = [m.sb(f"token{c}", [P, B, 2, MAX_TILES], BF16) for c in (0, 1)]
        part = m.sb("part", [P, 2, MAX_TILES])
        ps_before = m.ps("before", [P, NT, NE])
        ps_total = m.ps("total", [P, NT, NE])
        ps_token = m.ps("token", [P, 512])
        s, e_in, e_out, ranked, summed, hot_done, token_done = m.sems(
            "dve_step exp_in exp_out ranked summed hot_done token_done")
        block = stack.enter_context(nc.Block())

        @block.scalar
        def _(act):
            act.wait_ge(e_in, 1)
            act.activation(ex[:], ex[:], ACT.Exp).then_inc(e_out, 1)
            act.wait_ge(e_in, 2)
            act.activation(ediff[:], ediff[:], ACT.Exp).then_inc(e_out, 1)

        @block.tensor
        def _(pe):
            pe.wait_ge(ranked, 1)
            for h in (0, 1):
                tt = slice(h * NT // 2, (h + 1) * NT // 2)
                pe.matmul(ps_before[:, tt, :], C.before[:], both[:, tt, :], start=True, stop=True)
                mm = pe.matmul(ps_total[:, tt, :], C.ones[:], both[:, tt, :], start=True, stop=True)
            mm.then_inc(summed, 1)
            for b in range(2 * NT // B):
                pe.wait_ge(hot_done, b + 1)
                for j in range(B):
                    mm = pe.matmul(ps_token[:, 0:2 * MAX_TILES], is_lo[b % 2][:, j, :],
                                   token[b % 2][:, j, :, :].rearrange("p a b -> p (a b)"),
                                   start=b == 0 and j == 0, stop=b == 2 * NT // B - 1 and j == B - 1)
                mm.then_inc(token_done, 1)

        @block.vector
        def _(dve):
            n = [0]

            def link(ins):
                n[0] += 1
                ins.then_inc(s, 1)
                dve.wait_ge(s, n[0])

            L = C.logits
            link(dve.memset(gl[:], -3.0e38))
            link(dve.tensor_copy(gl[:, :, 0:NGRP], L[:, :, 0:NGRP]))
            for t in range(NT):
                dve.max(gmax[:, t, :], gl[:, t, :])
            link(dve.memset(C.zero[:], 0.0))
            for t in range(NT):
                dve.max_index(gidx[:, t, :], gmax[:, t, :], gl[:, t, :])
            link(dve.memset(C.zero[:], 0.0))
            dve.tensor_tensor(ex[:], gl[:, :, 0:NGRP], gmax[:, :, 0:1].to_broadcast([P, NT, NGRP]),
                              ALU.subtract).then_inc(e_in, 1)
            link(dve.tensor_copy(gsel[:], gidx[:, :, 0]))
            link(dve.tensor_tensor(pen[:], C.iota[:, 0:NGRP].unsqueeze(1).to_broadcast([P, NT, NGRP]),
                                   gsel[:].unsqueeze(2).to_broadcast([P, NT, NGRP]), ALU.is_equal))
            link(dve.tensor_scalar(pen[:], pen[:], -NEG, NEG, ALU.mult, ALU.add))
            link(dve.tensor_tensor(el[:].rearrange("p t (g e) -> p t g e", g=NGRP),
                                   L[:, :, NGRP:NLOG].rearrange("p t (g e) -> p t g e", g=NGRP),
                                   pen[:].unsqueeze(3).to_broadcast([P, NT, NGRP, EPG]), ALU.add))
            for t in range(NT):
                dve.max(emax[:, t, :], el[:, t, :])
            link(dve.memset(C.zero[:], 0.0))
            for t in range(NT):
                dve.max_index(eidx[:, t, :], emax[:, t, :], el[:, t, :])
            link(dve.memset(C.zero[:], 0.0))
            dve.tensor_tensor(ediff[:], emax[:, :, 1], emax[:, :, 0], ALU.subtract).then_inc(e_in, 1)
            for c in (0, 1):
                link(dve.tensor_copy(esel[:, c, :], eidx[:, :, c]))
                link(dve.tensor_tensor(one_hot[c][:], C.iota[:, 0:NE].unsqueeze(1).to_broadcast([P, NT, NE]),
                                       esel[:, c, :].unsqueeze(2).to_broadcast([P, NT, NE]), ALU.is_equal))
            dve.tensor_tensor(both[:], one_hot[0][:], one_hot[1][:], ALU.add).then_inc(ranked, 1)
            dve.wait_ge(e_out, 1)
            link(dve.reduce_sum(esum[:], ex[:], axis=AX_X))
            dve.wait_ge(e_out, 2)
            link(dve.tensor_scalar(den[:], ediff[:], 1.0, None, ALU.add))
            link(dve.tensor_tensor(den[:], den[:], esum[:], ALU.mult))
            link(dve.reciprocal(C.gates[:, 0, :], den[:]))
            link(dve.tensor_tensor(C.gates[:, 1, :], C.gates[:, 0, :], ediff[:], ALU.mult))
            dve.wait_ge(summed, 1)
            dve.tensor_copy(total[:], ps_total[:])
            link(dve.tensor_copy(scan[0][:], ps_total[:]))
            a = 0
            step = 1
            while step < NT:
                dve.tensor_copy(scan[1 - a][:, 0:step, :], scan[a][:, 0:step, :])
                link(dve.tensor_tensor(scan[1 - a][:, step:NT, :], scan[a][:, step:NT, :], scan[a][:, 0:NT - step, :], ALU.add))
                a, step = 1 - a, 2 * step
            link(dve.tensor_copy(tiles_i[:], scan[a][:, NT - 1, :]))
            link(dve.tensor_scalar(tiles_f[2][:], scan[a][:, NT - 1, :], float(P - 1), None, ALU.add))
            link(dve.tensor_copy(tiles_i[:], tiles_f[2][:]))
            link(dve.tensor_scalar(tiles_i[:], tiles_i[:], 7, None, ALU.arith_shift_right))
            link(dve.tensor_copy(tiles_f[2][:], tiles_i[:]))
            link(dve.tensor_scalar(tiles_f[2][:], tiles_f[2][:], 1.0, None, ALU.max))
            link(dve.tensor_copy(tiles_f[0][:], tiles_f[2][:]))
            b, step = 0, 1
            while step < NE:
                dve.tensor_copy(tiles_f[1 - b][:, 0:step], tiles_f[b][:, 0:step])
                link(dve.tensor_tensor(tiles_f[1 - b][:, step:NE], tiles_f[b][:, step:NE], tiles_f[b][:, 0:NE - step], ALU.add))
                b, step = 1 - b, 2 * step
            link(dve.memset(ends_f[:, 0:1], 0.0))
            link(dve.tensor_copy(ends_f[:, 1:NE + 1], tiles_f[b][:]))
            link(dve.tensor_copy(C.ends[:], ends_f[0:1, :]))
            link(dve.tensor_tensor(scan[a][:], scan[a][:], total[:], ALU.subtract))
            link(dve.tensor_tensor(scan[a][:], scan[a][:], ps_before[:], ALU.add))
            link(dve.scalar_tensor_tensor(out=scan[a][:], in0=ends_f[:, 0:NE].unsqueeze(1).to_broadcast([P, NT, NE]),
                                          scalar=float(P), in1=scan[a][:], op0=ALU.mult, op1=ALU.add))
            for c in (0, 1):
                link(dve.tensor_tensor(scan[1 - a][:], scan[a][:], one_hot[c][:], ALU.mult))
                link(dve.reduce_sum(slot_f[:, c, :], scan[1 - a][:], axis=AX_X))
            link(dve.tensor_copy(slot_i[:], slot_f[:]))
            link(dve.tensor_scalar(slot_f[:], slot_f[:], float(P), None, ALU.add))
            link(dve.tensor_copy(C.slot_row[:], slot_f[:]))
            flat = slot_i[:].rearrange("p c t -> p (c t)")
            link(dve.tensor_scalar(lo_i[:], flat, P - 1, None, ALU.bitwise_and))
            link(dve.tensor_scalar(hi_i[:], flat, 7, None, ALU.arith_shift_right))
            link(dve.tensor_copy(lo_f[:], lo_i[:]))
            link(dve.tensor_copy(hi_f[:], hi_i[:]))
            for b8 in range(2 * NT // B):
                w = b8 % 2
                cols = slice(b8 * B, (b8 + 1) * B)
                wait(dve, token_done, b8 - 1)
                t0 = b8 * B % NT
                dve.tensor_tensor(is_lo[w][:], C.iota[:].unsqueeze(1).to_broadcast([P, B, P]),
                                  lo_f[:, cols].unsqueeze(2).to_broadcast([P, B, P]), ALU.is_equal)
                link(dve.tensor_tensor(is_hi[w][:], C.iota[:, 0:MAX_TILES].unsqueeze(1).to_broadcast([P, B, MAX_TILES]),
                                       hi_f[:, cols].unsqueeze(2).to_broadcast([P, B, MAX_TILES]), ALU.is_equal))
                dve.tensor_scalar(token[w][:, :, 0, :], is_hi[w][:], C.lane[:, 0:1], None, ALU.mult)
                link(dve.tensor_tensor(token[w][:, :, 1, :], is_hi[w][:],
                                       C.iota[:, t0:t0 + B].unsqueeze(2).to_broadcast([P, B, MAX_TILES]), ALU.mult))
                dve.sem_inc(hot_done, 1)
            dve.wait_ge(token_done, 2 * NT // B)
            link(dve.tensor_copy(part[:].rearrange("p a b -> p (a b)"), ps_token[:, 0:2 * MAX_TILES]))
            link(dve.scalar_tensor_tensor(out=part[:, 0, :], in0=part[:, 1, :], scalar=float(P), in1=part[:, 0, :],
                                          op0=ALU.mult, op1=ALU.add))
            dve.memset(C.slot_token[:, MAX_TILES:MAX_TILES + 1], 0)
            link(dve.tensor_copy(C.slot_token[:, 0:MAX_TILES], part[:, 0, :]))


def experts_phase(nc, A, C, layer):
    with ExitStack() as stack:
        m = Mem(nc, f"ex{layer}", stack)
        raw = m.sb("raw", [P, NCHUNK, WCHUNK])
        w_hi = [m.sb(f"w_hi{u}", [P, NCHUNK * WCHUNK], BF16) for u in (0, 1)]
        w_lo = [m.sb(f"w_lo{u}", [P, NCHUNK * WCHUNK], BF16) for u in (0, 1)]
        token = m.sb("token", [P, 1], I32)
        xrow = m.sb("xrow", [P, 2 * D], BF16)
        xT = m.sb("xT", [P, 2, KD, P], BF16)
        silu = m.sb("silu", [P, F])
        a32 = m.sb("a32", [P, F])
        a = m.sb("a", [P, 2, F], BF16)
        aT = m.sb("aT", [P, 2, KF, P], BF16)
        y = m.sb("y", [P, D])
        ps_gate = m.ps("gate", [P, F])
        ps_up = [m.ps(f"up{h}", [P, 512]) for h in (0, 1)]
        ps_xT = m.ps("xT", [P, 2, KD, P], BF16)
        turned = "p (h k n) -> p h k n"
        ps_aT = [m.ps("aT", [P, 2, KF // 2, P], BF16)[:],
                 ps_up[0][:, F // 2:512].bitcast(BF16).rearrange(turned, h=2, k=KF // 2)]
        ps_y = m.ps("y", [P, D])
        raw_loaded = [m.sem(f"raw_loaded{c}") for c in range(NCHUNK)]
        hi_done, pool_lo, dve_lo, token_done, token_seen, gathered, xT_mm, xT_done = m.sems(
            "hi_done pool_lo dve_lo token_done token_seen gathered xT_mm xT_done")
        gate_mm, silu_done, up_mm, a_mul, a_done = m.sems("gate_mm silu_done up_mm a_mul a_done")
        aT_mm, aT_done, down_mm, y_done, y_stored, last_stored = m.sems("aT_mm aT_done down_mm y_done y_stored last_stored")
        halves = "l e (h k p) n -> (l e h) p k n"
        src = [A[n].rearrange(halves, p=P, k=WCHUNK // w) for n, w in (("w_exp_gate", F), ("w_exp_up", F), ("w_exp_down", D))]
        y_t = C.y_rows.rearrange("(t p) d -> t p d", p=P)
        block = stack.enter_context(nc.Block())

        def bounds(eng, e):
            return (eng.value_load(C.ends[0:1, bass.ds(e, 1)], min_val=0, max_val=MAX_TILES - 2),
                    eng.value_load(C.ends[0:1, bass.ds(e + 1, 1)], min_val=1, max_val=MAX_TILES - 1))

        def wait_split(eng, e, c):
            if c < POOL_CHUNKS:
                eng.wait_ge(pool_lo, POOL_CHUNKS * e + c + 1)
            else:
                eng.wait_ge(dve_lo, (NCHUNK - POOL_CHUNKS) * e + c - POOL_CHUNKS + 1)

        def lo_part(eng, e, u, c, lo_done):
            eng.wait_ge(hi_done, NCHUNK * e + c + 1)
            w = slice(c * WCHUNK, (c + 1) * WCHUNK)
            eng.tensor_tensor(w_lo[u][:, w], raw[:, c, :], w_hi[u][:, w], ALU.subtract).then_inc(lo_done, 1)

        @block.sync
        def _(sp):
            def load(e, c):
                part, half = divmod(c, 2)
                ap = src[part][layer * 2 * NE + 2 * e + half]
                sp.dma_start(raw[:, c, :].rearrange("p (k n) -> p k n", k=ap.shape[1]), ap).then_inc(raw_loaded[c], 16)

            for c in range(NCHUNK):
                load(0, c)
            with sp.Fori(0, NE - 1) as e:
                for c in range(NCHUNK):
                    wait_split(sp, e, c)
                    load(e + 1, c)

        @block.scalar
        def _(act):
            def split(e, u):
                if not isinstance(e, int):
                    ends = act.value_load(C.ends[0:1, bass.ds(e - 1, 1)], min_val=1, max_val=MAX_TILES - 1)
                for c in range(NCHUNK):
                    act.wait_ge(raw_loaded[c], 16 * (e + 1))
                    if not isinstance(e, int):
                        act.wait_ge((gate_mm, up_mm, down_mm)[c // 2], ends * (1, 2, 2)[c // 2])
                    act.activation(w_hi[u][:, c * WCHUNK:(c + 1) * WCHUNK], raw[:, c, :], ACT.Copy).then_inc(hi_done, 1)

            def store(k, stored):
                act.wait_ge(y_done, 2 * k + 4)
                act.dma_start(y_t[k + 1], y[:]).then_inc(stored, 16)

            def tiles(e):
                first, end = bounds(act, e)
                with act.Fori(first, end) as k:
                    act.wait_ge(gate_mm, k + 1)
                    act.activation(silu[:], ps_gate[:], ACT.Silu).then_inc(silu_done, 1)
                    store(k - 1, y_stored)
                return end

            split(0, 0)
            split(1, 1)
            tiles(0)
            with act.Fori(0, NE // 2 - 1) as i:
                for u in (0, 1):
                    split(2 * i + u + 2, u)
                    tiles(2 * i + u + 1)
            end = tiles(NE - 1)
            store(end - 1, last_stored)
            act.wait_ge(last_stored, 16)

        @block.gpsimd
        def _(pool):
            def split(e, u):
                for c in range(POOL_CHUNKS):
                    lo_part(pool, e, u, c, pool_lo)

            def gather(k):
                at = slice(k, k + 1) if isinstance(k, int) else bass.ds(k, 1)
                pool.tensor_copy(token[:], C.slot_token[:, at]).then_inc(token_done, 1)
                pool.wait_ge(token_done, k + 1)
                pool.sem_inc(token_seen, 1)
                pool.indirect_dma_start(xrow[:], None, C.hn_rows, bass.IndirectOffsetOnAxis(ap=token[:, 0:1], axis=0)).then_inc(gathered, 16)

            def tiles(e):
                first, end = bounds(pool, e)
                with pool.Fori(first, end) as k:
                    pool.wait_ge(xT_mm, k + 2)
                    gather(k + 2)
                return end

            gather(0)
            pool.wait_ge(xT_mm, 1)
            gather(1)
            split(0, 0)
            split(1, 1)
            tiles(0)
            with pool.Fori(0, NE // 2 - 1) as i:
                for u in (0, 1):
                    split(2 * i + u + 2, u)
                    tiles(2 * i + u + 1)
            end = tiles(NE - 1)
            pool.wait_ge(gathered, end * 16 + 32)

        @block.vector
        def _(dve):
            def split(e, u):
                for c in range(POOL_CHUNKS, NCHUNK):
                    lo_part(dve, e, u, c, dve_lo)

            def take_x(k):
                dve.wait_ge(xT_mm, k + 1)
                dve.tensor_copy(xT[:], ps_xT[:]).then_inc(xT_done, 1)

            def tiles(e):
                first, end = bounds(dve, e)
                with dve.Fori(first, end) as k:
                    dve.wait_ge(silu_done, k + 1)
                    for h in (0, 1):
                        c = slice(h * F // 2, (h + 1) * F // 2)
                        dve.wait_ge(up_mm, 2 * k + h + 1)
                        dve.tensor_tensor(a[:, 0, c], silu[:, c], ps_up[h][:, 0:F // 2], ALU.mult)
                        dve.tensor_tensor(a32[:, c], silu[:, c], ps_up[h][:, 0:F // 2], ALU.mult).then_inc(a_mul, 1)
                        dve.wait_ge(a_mul, 2 * k + h + 1)
                        dve.tensor_tensor(a[:, 1, c], a32[:, c], a[:, 0, c], ALU.subtract).then_inc(a_done, 1)
                        j = slice(h * KF // 2, (h + 1) * KF // 2)
                        dve.wait_ge(aT_mm, 2 * k + h + 1)
                        dve.tensor_copy(aT[:, :, j, :], ps_aT[h]).then_inc(aT_done, 1)
                    take_x(k + 1)
                    dve.wait_ge(y_stored, 16 * k + 16)
                    for n in (0, 1):
                        dve.wait_ge(down_mm, 2 * k + n + 1)
                        c = slice(512 * n, 512 * n + 512)
                        dve.tensor_copy(y[:, c], ps_y[:, c]).then_inc(y_done, 1)

            dve.memset(y[:], 0.0).then_inc(y_done, 2)
            take_x(0)
            split(0, 0)
            split(1, 1)
            tiles(0)
            with dve.Fori(0, NE // 2 - 1) as i:
                for u in (0, 1):
                    split(2 * i + u + 2, u)
                    tiles(2 * i + u + 1)
            tiles(NE - 1)

        @block.tensor
        def _(pe):
            def turn_x(k):
                pe.wait_ge(gathered, 16 * k + 16)
                for h in (0, 1):
                    for j in range(KD):
                        mm = pe.transpose(ps_xT[:, h, j, :], xrow[:, h * D + j * P:h * D + (j + 1) * P], C.ident_bf[:])
                mm.then_inc(xT_mm, 1)

            def turn_a(k, h):
                pe.wait_ge(a_done, 2 * k + h + 1)
                for part in (0, 1):
                    for i in range(KF // 2):
                        j = h * KF // 2 + i
                        mm = pe.transpose(ps_aT[h][:, part, i, :], a[:, part, j * P:(j + 1) * P], C.ident_bf[:])
                mm.then_inc(aT_mm, 1)

            def into_f(ps, u, part, c, rows):
                for j in rows:
                    w = slice((part * KD + j) * F + c.start, (part * KD + j) * F + c.stop)
                    mm = mm3(pe, ps, xT[:, 0, j, :], xT[:, 1, j, :], w_hi[u][:, w], w_lo[u][:, w], j == 0, j == KD - 1)
                return mm

            def down(u, h, n):
                for j in range(h * KF // 2, (h + 1) * KF // 2):
                    w = slice(2 * KD * F + j * D + n * 512, 2 * KD * F + j * D + (n + 1) * 512)
                    mm = mm3(pe, ps_y[:, n * 512:(n + 1) * 512], aT[:, 0, j, :], aT[:, 1, j, :], w_hi[u][:, w],
                             w_lo[u][:, w], j == 0, j == KF - 1)
                return mm

            turn_x(0)

            def tiles(e, u):
                first, end = bounds(pe, e)
                with pe.Fori(first, end) as k:
                    pe.wait_ge(xT_done, k + 1)
                    turn_x(k + 1)
                    wait_split(pe, e, 1)
                    into_f(ps_gate[:], u, 0, slice(0, F), range(KD)).then_inc(gate_mm, 1)
                    wait_split(pe, e, 2)
                    wait_split(pe, e, 3)
                    into_f(ps_up[0][:, 0:F // 2], u, 1, slice(0, F // 2), range(KD)).then_inc(up_mm, 1)
                    into_f(ps_up[1][:, 0:F // 2], u, 1, slice(F // 2, F), range(KD - 2))
                    turn_a(k, 0)
                    into_f(ps_up[1][:, 0:F // 2], u, 1, slice(F // 2, F), range(KD - 2, KD)).then_inc(up_mm, 1)
                    wait_split(pe, e, NCHUNK - 1)
                    pe.wait_ge(y_done, 2 * k + 2)
                    pe.wait_ge(aT_done, 2 * k + 1)
                    down(u, 0, 0)
                    turn_a(k, 1)
                    down(u, 0, 1)
                    pe.wait_ge(aT_done, 2 * k + 2)
                    down(u, 1, 0).then_inc(down_mm, 1)
                    down(u, 1, 1).then_inc(down_mm, 1)

            with pe.Fori(0, NE // 2) as i:
                for u in (0, 1):
                    tiles(2 * i + u, u)


def split_weights(nc, C, tag, gains, jobs):
    depth = 4
    with ExitStack() as stack:
        m = Mem(nc, tag, stack)
        width = max(job[2].shape[1] for job in jobs)
        raw = [m.sb(f"raw{i}", [P, width]) for i in range(depth)]
        raw_loaded = [m.sem(f"raw_loaded{i}") for i in range(depth)]
        gain_loaded, gain_done, hi_done, lo_done = m.sems("gain_loaded gain_done hi_done lo_done")
        block = stack.enter_context(nc.Block())

        @block.sync
        def _(sp):
            with nc.allow_non_contiguous_dma(reason="one gain per partition, once"):
                for vec, _, gain in gains:
                    sp.dma_start(gain, vec.rearrange("(k p) -> p k", p=P)).then_inc(gain_loaded, 16)
            for n, (sources, _, hi, _) in enumerate(jobs):
                wait(sp, lo_done, n - depth + 1)
                for parts, rows in sources:
                    sp.dma_start(raw[n % depth][parts, 0:hi.shape[1]], rows).then_inc(raw_loaded[n % depth], 16)

        loads = [0] * depth
        landed = []
        for n, (sources, _, _, _) in enumerate(jobs):
            loads[n % depth] += 16 * len(sources)
            landed.append(loads[n % depth])

        @block.scalar
        def _(act):
            wait(act, gain_done, len(gains))
            for n, (_, gain, hi, _) in enumerate(jobs):
                act.wait_ge(raw_loaded[n % depth], landed[n])
                act.activation(hi, raw[n % depth][:, 0:hi.shape[1]], ACT.Copy,
                               scale=1.0 if gain is None else gain).then_inc(hi_done, 1)

        @block.vector
        def _(dve):
            wait(dve, gain_loaded, 16 * len(gains))
            for _, factor, gain in gains:
                dve.tensor_scalar(gain, gain, factor, None, ALU.mult).then_inc(gain_done, 1)
            wait(dve, gain_done, len(gains))
            for n, (_, gain, hi, lo) in enumerate(jobs):
                dve.wait_ge(hi_done, n + 1)
                src = raw[n % depth][:, 0:hi.shape[1]]
                dve.scalar_tensor_tensor(out=lo, in0=src, scalar=1.0 if gain is None else gain, in1=hi,
                                         op0=ALU.mult, op1=ALU.subtract).then_inc(lo_done, 1)


def rotary_tables(nc, A, C, cos, sin):
    magic = float(1.5 * 2 ** 23)
    two_pi = 2 * np.pi
    c1 = 6.28125
    c2 = float(np.floor((two_pi - c1) * 2 ** 21) / 2 ** 21)
    c3 = float(np.float32(two_pi - c1 - c2))
    edge = float(np.nextafter(np.float32(np.pi), np.float32(0)))
    if edge > np.pi:
        edge = float(np.nextafter(np.float32(edge), np.float32(0)))
    nf = HEAD // 2
    with ExitStack() as stack:
        m = Mem(nc, "rot", stack)
        pos_i = m.sb("pos_i", [P, NT], I32)
        pos = m.sb("pos", [P, NT])
        inv = m.sb("inv", [P, nf])
        turns = m.sb("turns", [P, NT, nf])
        loaded, step_done, ready = m.sems("loaded step_done ready")
        block = stack.enter_context(nc.Block())

        @block.sync
        def _(sp):
            with nc.allow_non_contiguous_dma(reason="one position per partition, once"):
                sp.dma_start(pos_i[:], A["positions"][0].rearrange("(t p) -> p t", p=P)).then_inc(loaded, 16)

        @block.scalar
        def _(act):
            act.wait_ge(ready, 1)
            act.activation(sin[:], sin[:], ACT.Sin)
            act.activation(cos[:], cos[:], ACT.Sin)

        @block.vector
        def _(dve):
            n = [0]

            def link(ins):
                n[0] += 1
                ins.then_inc(step_done, 1)
                dve.wait_ge(step_done, n[0])

            for j in range(nf):
                dve.memset(inv[:, j:j + 1], float(INV_FREQ[j]))
            dve.wait_ge(loaded, 16)
            link(dve.tensor_copy(pos[:], pos_i[:]))
            shape = [P, NT, nf]
            link(dve.tensor_tensor(sin[:], pos[:].unsqueeze(2).to_broadcast(shape), inv[:].unsqueeze(1).to_broadcast(shape), ALU.mult))
            link(dve.tensor_scalar(turns[:], sin[:], 1.0 / two_pi, magic, ALU.mult, ALU.add))
            link(dve.tensor_scalar(turns[:], turns[:], -magic, None, ALU.add))
            for c in (c1, c2, c3):
                link(dve.scalar_tensor_tensor(out=sin[:], in0=turns[:], scalar=-c, in1=sin[:], op0=ALU.mult, op1=ALU.add))
            link(dve.tensor_scalar(turns[:], sin[:], float(np.pi / 2), -two_pi, ALU.is_gt, ALU.mult))
            link(dve.scalar_tensor_tensor(out=cos[:], in0=sin[:], scalar=float(np.pi / 2), in1=turns[:], op0=ALU.add, op1=ALU.add))
            link(dve.tensor_scalar(cos[:], cos[:], edge, -edge, ALU.min, ALU.max))
            dve.tensor_scalar(sin[:], sin[:], edge, -edge, ALU.min, ALU.max).then_inc(ready, 1)


def done(t, u):
    return 16 * ((t - u) // 2 + 1) if isinstance(t, int) else t * 8 + (16 - 8 * u)


def combine_phase(nc, A, C, layer, out):
    qkv = layer == 0
    with ExitStack() as stack:
        m = Mem(nc, f"cb{layer}", stack)
        wg = m.sb("wg", [P, 2, KD, D], BF16)
        wu = m.sb("wu", [P, 2, KPLE, D], BF16)
        g_ple = m.sb("g_ple", [P, KD])
        gains = [(A["g_ple"][layer], 1.0, g_ple[:])]
        rows = lambda w, k: [(slice(0, P), w[k * P:(k + 1) * P, :])]
        jobs = [(rows(A["w_ple_gate"][layer], k), g_ple[:, k:k + 1], wg[:, 0, k, :], wg[:, 1, k, :]) for k in range(KD)]
        jobs += [(rows(A["w_ple_up"][layer], k), None, wu[:, 0, k, :], wu[:, 1, k, :]) for k in range(KPLE)]
        if qkv:
            wq = m.sb("wq", [P, 2, KD, D], BF16)
            wkv = m.sb("wkv", [P, 2, KD, 2 * KVW], BF16)
            g_q = m.sb("g_q", [P, KD])
            g_kv = m.sb("g_kv", [P, KD])
            cos = m.sb("cos", [P, NT, HEAD // 2])
            sin = m.sb("sin", [P, NT, HEAD // 2])
            gains += [(A["g_mix"][1], HEAD ** -0.5, g_q[:]), (A["g_kv"], 1.0, g_kv[:])]
            jobs += [(rows(A["w_q"][0], k), g_q[:, k:k + 1], wq[:, 0, k, :], wq[:, 1, k, :]) for k in range(KD)]
            for w, at in (("w_k", 0), ("w_v", KVW)):
                jobs += [(rows(A[w], k), g_kv[:, k:k + 1], wkv[:, 0, k, at:at + KVW], wkv[:, 1, k, at:at + KVW])
                         for k in range(KD)]
            rotary_tables(nc, A, C, cos, sin)
        split_weights(nc, C, f"cw{layer}", gains, jobs)

        g_final = None if qkv else m.sb("g_final", [P, D])
        slot = [m.sb(f"slot{u}", [P, 2], I32) for u in (0, 1)]
        hin = [m.sb(f"hin{u}", [P, D]) for u in (0, 1)]
        y0 = [m.sb(f"y0_{u}", [P, D]) for u in (0, 1)]
        y1 = [m.sb(f"y1_{u}", [P, D]) for u in (0, 1)]
        p_in = [m.sb(f"p_in{u}", [P, PLE]) for u in (0, 1)]
        h2 = [m.sb(f"h2_{u}", [P, D]) for u in (0, 1)]
        x = m.sb("x", [P, 2, D], BF16)
        ph = m.sb("ph", [P, 2, PLE], BF16)
        xT = [m.sb(f"xT{u}", [P, 2, KD, P], BF16) for u in (0, 1)]
        pT = [m.sb(f"pT{u}", [P, 2, KPLE, P], BF16) for u in (0, 1)]
        th = m.sb("th", [P, 2, 512])
        mid = m.sb("mid", [P, 2, 512])
        h3 = [m.sb(f"h3_{u}", [P, D]) for u in (0, 1)]
        junk = m.sb("junk", [P, D])
        ss2, ms2, rs2, ss3, ms3, rs3 = (m.sb(n, [P, 1]) for n in ("ss2", "ms2", "rs2", "ss3", "ms3", "rs3"))
        if qkv:
            x3 = m.sb("x3", [P, 2, D], BF16)
            x3T = m.sb("x3T", [P, 2, KD, P], BF16)
            ra = m.sb("ra", [P, 512])
            rb = m.sb("rb", [P, 512])
            q_out = m.sb("q_out", [P, D])
            kv_out = m.sb("kv_out", [P, 2 * KVW])
        else:
            o_out = [m.sb(f"o_out{u}", [P, D]) for u in (0, 1)]
        ps_x = m.ps("x", [P, 2, KD, P], BF16)
        ps_p = m.ps("p", [P, 2, KPLE, P], BF16)
        ps = [m.ps(f"b{i}", [P, 512]) for i in range(5)]
        ps_gate, ps_up = (ps[0], ps[2]), (ps[1], ps[3])
        ps_q, ps_kv = (ps[4], ps[0]), ps[1]
        g_loaded = m.sem("g_loaded")
        h_ld, p_ld, y_ld, h3_st, o_st = ([m.sem(f"{n}{u}") for u in (0, 1)] for n in ("h_ld", "p_ld", "y_ld", "h3_st", "o_st"))
        slot_done, slot_seen, part_done, h2_done, ss2_done, ms2_done, rs2_done = m.sems("slot_done slot_seen part_done h2_done ss2_done ms2_done rs2_done")
        xh_done, xl_done, ph_done, pl_done, x_mm, xT_done, pT_done = m.sems("xh_done xl_done ph_done pl_done x_mm xT_done pT_done")
        gate_mm, up_mm, th_done, mid_done, h3_done = m.sems("gate_mm up_mm th_done mid_done h3_done")
        ss3_done, ms3_done, rs3_done, x3h_done, x3l_done, x3_mm, x3T_done = m.sems("ss3_done ms3_done rs3_done x3h_done x3l_done x3_mm x3T_done")
        q_mm, kv_mm, v_done, rot_mul, rot_add, o_done, q_st = m.sems("q_mm kv_mm v_done rot_mul rot_add o_done q_st")
        h_t = C.h_mid.rearrange("(t p) d -> t p d", p=P)
        p_t = A["p"][layer].rearrange("b (t p) d -> (b t) p d", p=P)
        h3_t = C.h_out.rearrange("(t p) d -> t p d", p=P)
        q_t = C.q_rows.rearrange("(t p) d -> t p d", p=P)
        kv_t = C.kv_rows.rearrange("(t p) d -> t p d", p=P)
        out_t = out.rearrange("b (t p) d -> (b t) p d", p=P)
        block = stack.enter_context(nc.Block())

        def steps(eng, step):
            step(-2, 0, True, False, False, False)
            step(-1, 1, True, True, False, False)
            step(0, 0, True, True, True, False)
            step(1, 1, True, True, True, True)
            with eng.Fori(1, NT // 2 - 1) as i:
                step(2 * i, 0, True, True, True, True)
                step(2 * i + 1, 1, True, True, True, True)
            step(NT - 2, 0, False, True, True, True)
            step(NT - 1, 1, False, False, True, True)
            step(NT, 0, False, False, False, True)

        @block.sync
        def _(sp):
            if not qkv:
                sp.dma_start(g_final[:], row(A["g_final"])).then_inc(g_loaded, 16)

            def step(s, u, load, head, mid_, tail):
                if load:
                    t = s + 2
                    wait(sp, h2_done, t - 1)
                    sp.dma_start(hin[u][:], h_t[t]).then_inc(h_ld[u], 16)
                    wait(sp, pl_done, t - 1)
                    sp.dma_start(p_in[u][:], p_t[t]).then_inc(p_ld[u], 16)
                if mid_ and qkv:
                    sp.wait_ge(h3_done, 2 * s + 2)
                    sp.dma_start(h3_t[s], h3[u][:]).then_inc(h3_st[u], 16)
                if tail and qkv:
                    t = s - 1
                    sp.wait_ge(rot_add, 3 * t + 3)
                    sp.dma_start(q_t[t], q_out[:]).then_inc(q_st, 16)
                    sp.wait_ge(v_done, t + 1)
                    sp.dma_start(kv_t[t], kv_out[:]).then_inc(q_st, 16)
                if tail and not qkv:
                    t = s - 1
                    sp.wait_ge(o_done, t + 1)
                    sp.dma_start(out_t[t], o_out[1 - u][:]).then_inc(o_st[1 - u], 16)

            steps(sp, step)
            if qkv:
                sp.wait_ge(q_st, 32 * NT)
                for u in (0, 1):
                    sp.wait_ge(h3_st[u], 8 * NT)
            else:
                for u in (0, 1):
                    sp.wait_ge(o_st[u], 8 * NT)

        @block.gpsimd
        def _(pool):
            def step(s, u, load, head, mid_, tail):
                if load:
                    t = s + 2
                    wait(pool, h2_done, t - 1)
                    at = slice(t, t + 1) if isinstance(t, int) else bass.ds(t, 1)
                    pool.tensor_copy(slot[u][:], C.slot_row[:, :, at].rearrange("p c t -> p (c t)")).then_inc(slot_done, 1)
                    pool.wait_ge(slot_done, t + 1)
                    pool.sem_inc(slot_seen, 1)
                    for c, y in enumerate((y0, y1)):
                        pool.indirect_dma_start(y[u][:], None, C.y_rows,
                                                bass.IndirectOffsetOnAxis(ap=slot[u][:, c:c + 1], axis=0)).then_inc(y_ld[u], 16)
                if head:
                    pool.wait_ge(ms2_done, s + 2)
                    wait(pool, xl_done, s + 1)
                    pool.tensor_tensor(rs2[:], ms2[:], C.minus_half[:], ALU.pow).then_inc(rs2_done, 1)
                if mid_:
                    pool.wait_ge(ms3_done, s + 1)
                    wait(pool, x3l_done if qkv else o_done, s)
                    pool.tensor_tensor(rs3[:], ms3[:], C.minus_half[:], ALU.pow).then_inc(rs3_done, 1)

            steps(pool, step)

        @block.scalar
        def _(act):
            def step(s, u, load, head, mid_, tail):
                v = 1 - u
                if head:
                    t = s + 1
                    act.wait_ge(p_ld[v], done(t, v))
                    wait(act, x_mm, t)
                    act.activation(ph[:, 0, :], p_in[v][:], ACT.Copy).then_inc(ph_done, 1)
                    act.wait_ge(h2_done, t + 1)
                    wait(act, ss3_done, s)
                    wait(act, ss2_done, t)
                    act.activation(junk[:], h2[v][:], ACT.Square, accum_out=ss2[:]).then_inc(ss2_done, 1)
                if head:
                    t = s + 1
                    act.wait_ge(rs2_done, t + 1)
                    act.activation(x[:, 0, :], h2[v][:], ACT.Copy, scale=rs2[:, 0:1]).then_inc(xh_done, 1)
                if mid_:
                    for h in (0, 1):
                        act.wait_ge(gate_mm, 2 * s + h + 1)
                        wait(act, mid_done, 2 * s + h - 1)
                        act.activation(th[:, h, :], ps_gate[h][:], ACT.Tanh, scale=0.5).then_inc(th_done, 1)
                    act.wait_ge(h3_done, 2 * s + 2)
                    wait(act, ss3_done, s)
                    wait(act, ss2_done, s + 2 if head else 0)
                    act.activation(junk[:], h3[u][:], ACT.Square, accum_out=ss3[:]).then_inc(ss3_done, 1)
                    if qkv:
                        act.wait_ge(rs3_done, s + 1)
                        wait(act, x3_mm, s)
                        act.activation(x3[:, 0, :], h3[u][:], ACT.Copy, scale=rs3[:, 0:1]).then_inc(x3h_done, 1)

            steps(act, step)

        @block.vector
        def _(dve):
            if not qkv:
                dve.wait_ge(g_loaded, 16)

            def rotate(t, at, src, dst, heads, n, mm, mm_count, pairs):
                nf = HEAD // 2
                shape = [P, heads, nf]
                c = cos[:, at, :].rearrange("p a f -> p (a f)").unsqueeze(1)
                sn = sin[:, at, :].rearrange("p a f -> p (a f)").unsqueeze(1)
                w = heads * HEAD
                dve.wait_ge(mm, mm_count)
                wait(dve, rot_add, 3 * t + n)
                dve.tensor_tensor(ra[:, 0:w].rearrange("p (h f) -> p h f", f=nf), src.rearrange("p (h f) -> p h f", f=nf),
                                  c.to_broadcast([P, 2 * heads, nf]), ALU.mult)
                s4 = src.rearrange("p (h two f) -> p h two f", two=2, f=nf)
                a4 = ra[:, 0:w].rearrange("p (h two f) -> p h two f", two=2, f=nf)
                b4 = rb[:, 0:w].rearrange("p (h two f) -> p h two f", two=2, f=nf)
                dve.tensor_tensor(b4[:, :, 0, :], s4[:, :, 1, :], sn.to_broadcast(shape), ALU.mult)
                dve.tensor_tensor(b4[:, :, 1, :], s4[:, :, 0, :], sn.to_broadcast(shape), ALU.mult).then_inc(rot_mul, 1)
                dve.wait_ge(rot_mul, 3 * t + n + 1)
                for half, op in ((0, ALU.subtract), (1, ALU.add)):
                    i0, i1 = a4[:, :, half, :], b4[:, :, half, :]
                    o = dst.rearrange("p (h two f) -> p h two f", two=2, f=nf)[:, :, half, :]
                    if pairs:
                        i0 = i0.rearrange("p (s i) f -> p s i f", s=2)
                        i1 = i1.rearrange("p (s i) f -> p s i f", s=2)
                        o = o.rearrange("p (i s) f -> p s i f", s=2)
                    last = dve.tensor_tensor(o, i0, i1, op)
                last.then_inc(rot_add, 1)

            def step(s, u, load, head, mid_, tail):
                v = 1 - u
                if head:
                    t = s + 1
                    at = slice(t, t + 1) if isinstance(t, int) else bass.ds(t, 1)
                    dve.wait_ge(h_ld[v], done(t, v))
                    dve.wait_ge(y_ld[v], 2 * done(t, v))
                    dve.scalar_tensor_tensor(out=h2[v][:], in0=y0[v][:], scalar=C.gates[:, 0, at], in1=hin[v][:],
                                             op0=ALU.mult, op1=ALU.add).then_inc(part_done, 1)
                    dve.wait_ge(part_done, t + 1)
                    dve.scalar_tensor_tensor(out=h2[v][:], in0=y1[v][:], scalar=C.gates[:, 1, at], in1=h2[v][:],
                                             op0=ALU.mult, op1=ALU.add).then_inc(h2_done, 1)
                    dve.wait_ge(ph_done, t + 1)
                    dve.tensor_tensor(ph[:, 1, :], p_in[v][:], ph[:, 0, :], ALU.subtract).then_inc(pl_done, 1)
                    dve.wait_ge(ss2_done, t + 1)
                    dve.tensor_scalar(ms2[:], ss2[:], 1.0 / D, EPS, ALU.mult, ALU.add).then_inc(ms2_done, 1)
                if tail and qkv:
                    t = s - 1
                    dve.wait_ge(x3_mm, t + 1)
                    wait(dve, kv_mm, t)
                    dve.tensor_copy(x3T[:], ps_x[:]).then_inc(x3T_done, 1)
                if tail and not qkv:
                    t = s - 1
                    dve.wait_ge(rs3_done, t + 1)
                    wait(dve, o_st[v], done(t - 2, v) if not isinstance(t, int) or t >= 2 else 0)
                    dve.scalar_tensor_tensor(out=o_out[v][:], in0=h3[v][:], scalar=rs3[:, 0:1], in1=g_final[:],
                                             op0=ALU.mult, op1=ALU.mult).then_inc(o_done, 1)
                if head:
                    t = s + 1
                    dve.wait_ge(xh_done, t + 1)
                    dve.scalar_tensor_tensor(out=x[:, 1, :], in0=h2[v][:], scalar=rs2[:, 0:1], in1=x[:, 0, :],
                                             op0=ALU.mult, op1=ALU.subtract).then_inc(xl_done, 1)

                def residual(h):
                    c = slice(512 * h, 512 * h + 512)
                    dve.wait_ge(th_done, 2 * s + h + 1)
                    dve.wait_ge(up_mm, 2 * s + h + 1)
                    wait(dve, h3_done, 2 * s + h - 1)
                    dve.scalar_tensor_tensor(out=mid[:, h, :], in0=th[:, h, :], scalar=1.0, in1=ps_up[h][:],
                                             op0=ALU.add, op1=ALU.mult).then_inc(mid_done, 1)
                    dve.wait_ge(mid_done, 2 * s + h + 1)
                    dve.scalar_tensor_tensor(out=h3[u][:, c], in0=mid[:, h, :], scalar=0.5, in1=h2[u][:, c],
                                             op0=ALU.mult, op1=ALU.add).then_inc(h3_done, 1)

                if mid_:
                    if qkv:
                        wait(dve, h3_st[u], done(s - 2, u) if not isinstance(s, int) or s >= 2 else 0)
                    residual(0)
                if mid_:
                    residual(1)
                if head:
                    t = s + 1
                    dve.wait_ge(x_mm, t + 1)
                    dve.tensor_copy(pT[v][:], ps_p[:]).then_inc(pT_done, 1)
                    dve.tensor_copy(xT[v][:], ps_x[:]).then_inc(xT_done, 1)
                if mid_:
                    dve.wait_ge(ss3_done, s + 1)
                    wait(dve, rs3_done, s)
                    dve.tensor_scalar(ms3[:], ss3[:], 1.0 / D, EPS, ALU.mult, ALU.add).then_inc(ms3_done, 1)
                if mid_ and qkv:
                    dve.wait_ge(x3h_done, s + 1)
                    dve.scalar_tensor_tensor(out=x3[:, 1, :], in0=h3[u][:], scalar=rs3[:, 0:1], in1=x3[:, 0, :],
                                             op0=ALU.mult, op1=ALU.subtract).then_inc(x3l_done, 1)
                if tail and qkv:
                    t = s - 1
                    at = slice(t, t + 1) if isinstance(t, int) else bass.ds(t, 1)
                    wait(dve, q_st, 32 * t)
                    for h in (0, 1):
                        rotate(t, at, ps_q[h][:], q_out[:, 512 * h:512 * h + 512], 8, h, q_mm, 2 * t + h + 1, True)
                    rotate(t, at, ps_kv[:, 0:KVW], kv_out[:, 0:KVW], NKV, 2, kv_mm, t + 1, False)
                    dve.tensor_copy(kv_out[:, KVW:2 * KVW], ps_kv[:, KVW:2 * KVW]).then_inc(v_done, 1)

            steps(dve, step)

        @block.tensor
        def _(pe):
            def product(dst, lhs, w, kk, c):
                for k in range(kk):
                    mm = mm3(pe, dst, lhs[:, 0, k, :], lhs[:, 1, k, :], w[:, 0, k, c], w[:, 1, k, c], k == 0, k == kk - 1)
                return mm

            def step(s, u, load, head, mid_, tail):
                v = 1 - u
                if tail and qkv:
                    t = s - 1
                    pe.wait_ge(x3l_done, t + 1)
                    if mid_:
                        pe.wait_ge(xT_done, s + 1)
                    for h in (0, 1):
                        for k in range(KD):
                            mm = pe.transpose(ps_x[:, h, k, :], x3[:, h, k * P:(k + 1) * P], C.ident_bf[:])
                    mm.then_inc(x3_mm, 1)

                def gate_up(h):
                    c = slice(512 * h, 512 * h + 512)
                    if qkv and h == 0:
                        wait(pe, rot_mul, 3 * (s - 2) + 2)
                    wait(pe, th_done, 2 * s + h - 1)
                    product(ps_gate[h][:], xT[u], wg, KD, c).then_inc(gate_mm, 1)
                    if qkv and h == 0:
                        wait(pe, rot_mul, 3 * (s - 2) + 3)
                        wait(pe, v_done, s - 1)
                    wait(pe, mid_done, 2 * s + h - 1)
                    product(ps_up[h][:], pT[u], wu, KPLE, c).then_inc(up_mm, 1)

                if mid_:
                    pe.wait_ge(xT_done, s + 1)
                    pe.wait_ge(pT_done, s + 1)
                    gate_up(0)
                    gate_up(1)
                if head:
                    t = s + 1
                    pe.wait_ge(xl_done, t + 1)
                    pe.wait_ge(pl_done, t + 1)
                    wait(pe, xT_done, t)
                    wait(pe, pT_done, t)
                    if qkv:
                        wait(pe, x3T_done, s if tail else 0)
                    for h in (0, 1):
                        for k in range(KPLE):
                            pe.transpose(ps_p[:, h, k, :], ph[:, h, k * P:(k + 1) * P], C.ident_bf[:])
                    for h in (0, 1):
                        for k in range(KD):
                            mm = pe.transpose(ps_x[:, h, k, :], x[:, h, k * P:(k + 1) * P], C.ident_bf[:])
                    mm.then_inc(x_mm, 1)
                if tail and qkv:
                    t = s - 1
                    pe.wait_ge(x3T_done, t + 1)
                    wait(pe, rot_mul, 3 * (t - 1) + 1)
                    product(ps_q[0][:], x3T, wq, KD, slice(0, 512)).then_inc(q_mm, 1)
                    if mid_:
                        pe.wait_ge(th_done, 2 * s + 1)
                    product(ps_q[1][:], x3T, wq, KD, slice(512, 1024)).then_inc(q_mm, 1)
                    if mid_:
                        pe.wait_ge(mid_done, 2 * s + 1)
                    product(ps_kv[:], x3T, wkv, KD, slice(0, 512)).then_inc(kv_mm, 1)

            steps(pe, step)


def attention_phase(nc, A, C):
    NP = NQ // 2
    with ExitStack() as stack:
        m = Mem(nc, "att", stack)
        wo = m.sb("wo", [P, 2, KD, D], BF16)
        src = A["w_o"][0].rearrange("(jj s i e) n -> jj i s e n", jj=2, s=2, i=4)
        jobs = [([(slice(0, HEAD), src[c // 4, c % 4, 0]), (slice(HEAD, P), src[c // 4, c % 4, 1])], None,
                 wo[:, 0, c, :], wo[:, 1, c, :]) for c in range(NP)]
        split_weights(nc, C, "aw", [], jobs)

        g_ffn = m.sb("g_ffn", [P, D])
        w_router = m.sb("w_router", [P, KD, NLOG])
        bias = m.sb("bias", [P, NLOG])
        sink = m.sb("sink", [P, NQ])
        mask = m.sb("mask", [P, 2 * P])
        q_in = [m.sb(f"q_in{u}", [P, D]) for u in (0, 1)]
        kv_in = [m.sb(f"kv_in{u}", [P, 2 * KVW]) for u in (0, 1)]
        h3 = [m.sb(f"h3_{u}", [P, D]) for u in (0, 1)]
        qT = m.sb("qT", [P, NP, P])
        kT = [m.sb(f"kT{u}", [P, 2, 2, P]) for u in (0, 1)]
        vv = [m.sb(f"v{u}", [P, KVW]) for u in (0, 1)]
        SR = 4
        score = [m.sb(f"score{i}", [P, 2, 2 * P]) for i in range(SR)]
        prT = [m.sb(f"prT{i}", [P, 4, P]) for i in range(2)]
        mx, nmx, esum, esink, den = (m.sb(n, [P, NQ]) for n in ("mx", "nmx", "esum", "esink", "den"))
        o32 = m.sb("o32", [P, D])
        o = m.sb("o", [P, 2, D], BF16)
        oT = m.sb("oT", [P, 2, KD, P], BF16)
        h4 = [m.sb(f"h4_{u}", [P, D]) for u in (0, 1)]
        hn = m.sb("hn", [P, D])
        hnT = m.sb("hnT", [P, KD, P])
        hrow = [m.sb(f"hrow{u}", [P, 2 * D], BF16) for u in (0, 1)]
        junk = m.sb("junk", [P, D])
        ss, ms, rs = (m.sb(n, [P, 1]) for n in ("ss", "ms", "rs"))
        ps_s = m.ps("s", [P, 2, 2, 2 * P])
        ps_p = m.ps("p", [P, 2, 4, P])
        ps_o = m.ps("o", [P, NQ, HEAD])
        ps_x = m.ps("x", [P, D])
        loaded, fixed = m.sems("loaded fixed")
        q_ld, kv_ld, h3_ld, h4_st, row_st = ([m.sem(f"{n}{u}") for u in (0, 1)] for n in ("q_ld", "kv_ld", "h3_ld", "h4_st", "row_st"))
        turn_mm, qT_done, kT_done, v_done, mask_done = m.sems("turn_mm qT_done kT_done v_done mask_done")
        s_mm, top_open, mx_done, nmx_done, e_done, pT_mm, pT_done, pv_mm = m.sems("s_mm top_open mx_done nmx_done e_done pT_mm pT_done pv_mm")
        diff_done, esink_done, den_done, rden_done, o_done, oh_done, ol_done, oT_mm, oT_done = m.sems(
            "diff_done esink_done den_done rden_done o_done oh_done ol_done oT_mm oT_done")
        wo_mm, h4_done, ss_done, ms_done, rs_done, hn_done, hi_done, lo_done, hnT_mm, hnT_done, log_mm, log_done = m.sems(
            "wo_mm h4_done ss_done ms_done rs_done hn_done hi_done lo_done hnT_mm hnT_done log_mm log_done")
        q_t = C.q_rows.rearrange("(t p) d -> t p d", p=P)
        kv_t = C.kv_rows.rearrange("(t p) d -> t p d", p=P)
        h3_t = C.h_out.rearrange("(t p) d -> t p d", p=P)
        h4_t = C.h_mid.rearrange("(t p) d -> t p d", p=P)
        row_t = C.hn_rows.rearrange("(t p) d -> t p d", p=P)
        block = stack.enter_context(nc.Block())

        def steps(eng, step):
            step(-1, 1, True, False, False)
            step(0, 0, True, True, False)
            step(1, 1, True, True, True)
            with eng.Fori(1, NT // 2 - 1) as i:
                step(2 * i, 0, True, True, True)
                step(2 * i + 1, 1, True, True, True)
            step(NT - 2, 0, True, True, True)
            step(NT - 1, 1, False, True, True)
            step(NT, 0, False, False, True)

        @block.sync
        def _(sp):
            with nc.allow_non_contiguous_dma(reason="sinks in head-pair order, once"):
                for jj in (0, 1):
                    for k in (0, 1):
                        sp.dma_start(sink[:, 8 * jj + k:8 * jj + 8:2],
                                     row(A["sinks"][0][8 * jj + 4 * k:8 * jj + 4 * k + 4])).then_inc(loaded, 16)
            sp.dma_start(g_ffn[:], row(A["g_ffn"][1])).then_inc(loaded, 16)
            load_router(nc, sp, A, w_router, bias, 1, loaded)

            def step(s, u, load, attend, tail):
                v = 1 - u
                if load:
                    t = s + 1
                    wait(sp, qT_done, t - 1)
                    sp.dma_start(q_in[v][:], q_t[t]).then_inc(q_ld[v], 16)
                    wait(sp, kT_done, t - 1)
                    wait(sp, v_done, t - 1)
                    sp.dma_start(kv_in[v][:], kv_t[t]).then_inc(kv_ld[v], 16)
                if tail:
                    t = s - 1
                    sp.wait_ge(h4_done, t + 1)
                    sp.dma_start(h4_t[t], h4[v][:]).then_inc(h4_st[v], 16)
                if load:
                    t = s + 1
                    wait(sp, h4_done, t - 1)
                    sp.dma_start(h3[v][:], h3_t[t]).then_inc(h3_ld[v], 16)
                if tail:
                    t = s - 1
                    sp.wait_ge(lo_done, t + 1)
                    sp.dma_start(row_t[t], hrow[v][:]).then_inc(row_st[v], 16)

            steps(sp, step)
            for u in (0, 1):
                sp.wait_ge(h4_st[u], 8 * NT)
                sp.wait_ge(row_st[u], 8 * NT)

        @block.gpsimd
        def _(pool):
            for u in (0, 1):
                pool.memset(kT[u][:], 0.0).then_inc(fixed, 1)
            pool.memset(vv[1][:], 0.0).then_inc(fixed, 1)

            def step(s, u, load, attend, tail):
                if tail:
                    pool.wait_ge(ms_done, s)
                    wait(pool, hn_done, s - 1)
                    pool.tensor_tensor(rs[:], ms[:], C.minus_half[:], ALU.pow).then_inc(rs_done, 1)

            steps(pool, step)

        @block.scalar
        def _(act):
            def step(s, u, load, attend, tail):
                v = 1 - u
                if attend:
                    act.wait_ge(turn_mm, s + 1)
                    wait(act, s_mm, NP * s)
                    act.activation(qT[:], ps_s[:].rearrange("p a b c -> p (a b c)"), ACT.Copy).then_inc(qT_done, 1)

                def exps(c):
                    b = c % SR
                    act.wait_ge(nmx_done, NP * s + c + 1)
                    for k in (0, 1):
                        n = 2 * c + k
                        e = act.activation(score[b][:, k, :], score[b][:, k, :], ACT.Exp, bias=nmx[:, n:n + 1],
                                           accum_out=esum[:, n:n + 1])
                    e.then_inc(e_done, 1)

                def tail_norm():
                    t = s - 1
                    act.wait_ge(h4_done, t + 1)
                    wait(act, ss_done, t)
                    act.activation(junk[:], h4[v][:], ACT.Square, accum_out=ss[:]).then_inc(ss_done, 1)

                def tail_hi():
                    t = s - 1
                    act.wait_ge(hn_done, t + 1)
                    wait(act, row_st[v], done(t - 2, v) if not isinstance(t, int) or t >= 2 else 0)
                    act.activation(hrow[v][:, 0:D], hn[:], ACT.Copy).then_inc(hi_done, 1)

                if attend:
                    for c in range(NP):
                        if c == 2 and tail:
                            tail_norm()
                        if c == 4 and tail:
                            tail_hi()
                        exps(c)
                elif tail:
                    tail_norm()
                    tail_hi()
                if tail:
                    t = s - 1
                    act.wait_ge(hnT_mm, t + 1)
                    wait(act, log_mm, t)
                    act.activation(hnT[:], ps_x[:], ACT.Copy).then_inc(hnT_done, 1)
                if attend:
                    act.wait_ge(diff_done, s + 1)
                    act.activation(esink[:], esink[:], ACT.Exp).then_inc(esink_done, 1)
                    act.wait_ge(o_done, s + 1)
                    wait(act, oT_mm, s)
                    act.activation(o[:, 0, :], o32[:], ACT.Copy).then_inc(oh_done, 1)

            steps(act, step)

        @block.vector
        def _(dve):
            dve.wait_ge(loaded, 16 * 9)

            def step(s, u, load, attend, tail):
                v = 1 - u
                if attend:
                    if isinstance(s, int) and s <= 1:
                        wait(dve, mx_done, NP * s)
                        dve.tensor_copy(mask[:], (C.mask_first if s == 0 else C.mask)[:]).then_inc(mask_done, 1)
                        dve.wait_ge(mask_done, s + 1)
                        dve.wait_ge(fixed, 3)
                    dve.wait_ge(turn_mm, s + 1)
                    wait(dve, s_mm, NP * s)
                    for k in (0, 1):
                        rows = slice(HEAD * k, HEAD * k + HEAD)
                        last = dve.tensor_copy(kT[u][rows, :, k, :], ps_p[rows, 0, 0:2, :])
                    last.then_inc(kT_done, 1)
                    dve.wait_ge(kv_ld[u], done(s, u))
                    wait(dve, pv_mm, NP * s)
                    dve.tensor_copy(vv[u][:], kv_in[u][:, KVW:2 * KVW]).then_inc(v_done, 1)
                if tail:
                    t = s - 1
                    dve.wait_ge(oT_mm, t + 1)
                    wait(dve, wo_mm, t)
                    dve.tensor_copy(oT[:], ps_x[:].bitcast(BF16).rearrange("p (h k n) -> p h k n", h=2, k=KD)).then_inc(oT_done, 1)

                def top(c):
                    b = c % SR
                    dve.wait_ge(s_mm, NP * s + c + 1)
                    wait(dve, pT_mm, NP * s + c + 1 - SR)
                    wait(dve, e_done, NP * s + c + 1 - NP)
                    dve.sem_inc(top_open, 1)
                    for k in (0, 1):
                        n = 2 * c + k
                        last = dve.tensor_tensor_reduce(out=score[b][:, k, :], in0=ps_s[:, c % 2, k, :], in1=mask[:],
                                                        scale=1.0, scalar=sink[:, n:n + 1], op0=ALU.add, op1=ALU.max,
                                                        accum_out=mx[:, n:n + 1])
                    last.then_inc(mx_done, 1)
                    dve.wait_ge(mx_done, NP * s + c + 1)
                    dve.tensor_scalar(nmx[:, 2 * c:2 * c + 2], mx[:, 2 * c:2 * c + 2], -1.0, None, ALU.mult).then_inc(nmx_done, 1)

                def turned(c):
                    dve.wait_ge(pT_mm, NP * s + c + 1)
                    wait(dve, pv_mm, NP * s + c - 1)
                    dve.tensor_copy(prT[c % 2][:], ps_p[:, c % 2, :, :]).then_inc(pT_done, 1)

                def tail_part(n):
                    t = s - 1
                    if n == 0:
                        dve.wait_ge(wo_mm, t + 1)
                        dve.wait_ge(h3_ld[v], done(t, v))
                        wait(dve, h4_st[v], done(t - 2, v) if not isinstance(t, int) or t >= 2 else 0)
                        dve.tensor_tensor(h4[v][:], ps_x[:], h3[v][:], ALU.add).then_inc(h4_done, 1)
                    if n == 1:
                        dve.wait_ge(ss_done, t + 1)
                        dve.tensor_scalar(ms[:], ss[:], 1.0 / D, EPS, ALU.mult, ALU.add).then_inc(ms_done, 1)
                    if n == 2:
                        dve.wait_ge(rs_done, t + 1)
                        wait(dve, hnT_mm, t)
                        dve.scalar_tensor_tensor(out=hn[:], in0=h4[v][:], scalar=rs[:, 0:1], in1=g_ffn[:],
                                                 op0=ALU.mult, op1=ALU.mult).then_inc(hn_done, 1)
                    if n == 3:
                        dve.wait_ge(hi_done, t + 1)
                        dve.wait_ge(hn_done, t + 1)
                        dve.tensor_tensor(hrow[v][:, D:2 * D], hn[:], hrow[v][:, 0:D], ALU.subtract).then_inc(lo_done, 1)

                if attend:
                    for c in range(NP + 2):
                        if c < NP:
                            top(c)
                        if c >= 2:
                            turned(c - 2)
                        if tail and c in (0, 2, 3, 5):
                            tail_part((0, 2, 3, 5).index(c))
                elif tail:
                    for n in range(4):
                        tail_part(n)
                if attend:
                    dve.tensor_tensor(esink[:], sink[:], nmx[:], ALU.add).then_inc(diff_done, 1)
                if tail:
                    t = s - 1
                    dve.wait_ge(log_mm, t + 1)
                    at = slice(t, t + 1) if isinstance(t, int) else bass.ds(t, 1)
                    dve.tensor_tensor(C.logits[:, at, :].rearrange("p a b -> p (a b)"),
                                      ps_p[:, 1, 0, 0:NLOG], bias[:], ALU.add).then_inc(log_done, 1)
                if attend:
                    dve.wait_ge(esink_done, s + 1)
                    dve.wait_ge(e_done, NP * s + NP)
                    dve.tensor_tensor(den[:], esum[:], esink[:], ALU.add).then_inc(den_done, 1)
                    dve.wait_ge(den_done, s + 1)
                    dve.reciprocal(den[:], den[:]).then_inc(rden_done, 1)
                    dve.wait_ge(rden_done, s + 1)
                    dve.wait_ge(pv_mm, NP * s + NP)
                    dve.tensor_tensor(o32[:].rearrange("p (n e) -> p n e", e=HEAD), ps_o[:],
                                      den[:].unsqueeze(2).to_broadcast([P, NQ, HEAD]), ALU.mult).then_inc(o_done, 1)
                    dve.wait_ge(oh_done, s + 1)
                    dve.wait_ge(o_done, s + 1)
                    dve.tensor_tensor(o[:, 1, :], o32[:], o[:, 0, :], ALU.subtract).then_inc(ol_done, 1)

            steps(dve, step)

        @block.tensor
        def _(pe):
            pe.wait_ge(loaded, 16 * 9)

            def step(s, u, load, attend, tail):
                v = 1 - u
                if tail:
                    t = s - 1
                    pe.wait_ge(ol_done, t + 1)
                    wait(pe, hnT_done, t)
                    x_bf = ps_x[:].bitcast(BF16)
                    for h in (0, 1):
                        for k in range(KD):
                            at = (h * KD + k) * P
                            mm = pe.transpose(x_bf[:, at:at + P], o[:, h, k * P:(k + 1) * P], C.ident_bf[:])
                    mm.then_inc(oT_mm, 1)
                if attend:
                    pe.wait_ge(q_ld[u], done(s, u))
                    pe.wait_ge(kv_ld[u], done(s, u))
                    wait(pe, mx_done, NP * s)
                    wait(pe, pT_done, NP * s)
                    wait(pe, log_done, s - 1)
                    flat = ps_s[:].rearrange("p a b c -> p (a b c)")
                    for c in range(NP):
                        pe.transpose(flat[:, c * P:(c + 1) * P], q_in[u][:, c * P:(c + 1) * P], C.ident[:])
                    for j in (0, 1):
                        mm = pe.transpose(ps_p[:, 0, j, :], kv_in[u][:, j * P:(j + 1) * P], C.ident[:])
                    mm.then_inc(turn_mm, 1)
                if tail:
                    t = s - 1
                    pe.wait_ge(oT_done, t + 1)
                    for n in (0, 1):
                        c = slice(512 * n, 512 * n + 512)
                        for k in range(KD):
                            mm = mm3(pe, ps_x[:, c], oT[:, 0, k, :], oT[:, 1, k, :], wo[:, 0, k, c], wo[:, 1, k, c],
                                     k == 0, k == KD - 1)
                    mm.then_inc(wo_mm, 1)

                def scores(c):
                    if c < 2:
                        pe.wait_ge(qT_done, s + 1)
                        pe.wait_ge(kT_done, s + 1)
                    wait(pe, mx_done, NP * s + c - 1)
                    jj = c // 4
                    for b, keys in ((0, kT[v]), (1, kT[u])):
                        mm = pe.matmul(ps_s[:, c % 2, :, b * P:(b + 1) * P], qT[:, c, :], keys[:, jj, :, :],
                                       start=True, stop=True)
                    mm.then_inc(s_mm, 1)

                def turn(c):
                    pe.wait_ge(e_done, NP * s + c + 1)
                    wait(pe, pT_done, NP * s + c - 1)
                    for k in (0, 1):
                        for b in (0, 1):
                            mm = pe.transpose(ps_p[:, c % 2, 2 * k + b, :], score[c % SR][:, k, b * P:(b + 1) * P], C.ident[:])
                    mm.then_inc(pT_mm, 1)

                def weigh(c):
                    pe.wait_ge(pT_done, NP * s + c + 1)
                    if c == 0:
                        pe.wait_ge(v_done, s + 1)
                        wait(pe, o_done, s)
                    for k in (0, 1):
                        kv = 2 * (c // 4) + k
                        cols = slice(kv * HEAD, kv * HEAD + HEAD)
                        for b, val in ((0, vv[v]), (1, vv[u])):
                            mm = pe.matmul(ps_o[:, 2 * c + k, :], prT[c % 2][:, 2 * k + b, :], val[:, cols],
                                           start=b == 0, stop=b == 1)
                    mm.then_inc(pv_mm, 1)

                if attend:
                    for c in range(NP + 3):
                        if c < NP:
                            scores(c)
                        if 2 <= c < NP + 2:
                            turn(c - 2)
                        if c >= 3:
                            weigh(c - 3)
                if tail:
                    t = s - 1
                    pe.wait_ge(hn_done, t + 1)
                    pe.wait_ge(h4_done, t + 1)
                    for k in range(KD):
                        mm = pe.transpose(ps_x[:, k * P:(k + 1) * P], hn[:, k * P:(k + 1) * P], C.ident[:])
                    mm.then_inc(hnT_mm, 1)
                    pe.wait_ge(hnT_done, t + 1)
                    if attend:
                        pe.wait_ge(pT_done, NP * s + NP)
                    for k in range(KD):
                        mm = pe.matmul(ps_p[:, 1, 0, 0:NLOG], hnT[:, k, :], w_router[:, k, :], start=k == 0, stop=k == KD - 1)
                    mm.then_inc(log_mm, 1)

            steps(pe, step)


class Shared:

    def __init__(self, nc, stack):
        m = Mem(nc, "all", stack)
        self.ident = m.sb("ident", [P, P])
        self.ident_bf = m.sb("ident_bf", [P, P], BF16)
        self.before = m.sb("before", [P, P])
        self.ones = m.sb("ones", [P, P])
        self.iota = m.sb("iota", [P, P])
        self.lane = m.sb("lane", [P, 1])
        self.minus_half = m.sb("minus_half", [P, 1])
        self.zero = m.sb("zero", [P, 1])
        self.band = m.sb("band", [P, len(WINDOWS), P])
        self.band_first = m.sb("band_first", [P, len(WINDOWS), P])
        self.band_prev = m.sb("band_prev", [P, len(WINDOWS), TAIL])
        self.mask = m.sb("mask", [P, 2 * P])
        self.mask_first = m.sb("mask_first", [P, 2 * P])
        self.logits = m.sb("logits", [P, NT, NLOG])
        self.gates = m.sb("gates", [P, 2, NT])
        self.slot_row = m.sb("slot_row", [P, 2, NT], I32)
        self.slot_token = m.sb("slot_token", [P, MAX_TILES + 1], I32)
        self.ends = m.sb("ends", [1, NE + 1], I32)
        dram = lambda name, shape, dt=F32: nc.dram_tensor(name, shape, dt, kind="Internal").ap()
        self.h_mid = dram("h_mid", [T, D])
        self.h_out = dram("h_out", [T, D])
        self.hn_rows = dram("hn_rows", [T, 2 * D], BF16)
        self.y_rows = dram("y_rows", [(MAX_TILES + 1) * P, D])
        self.q_rows = dram("q_rows", [T, D])
        self.kv_rows = dram("kv_rows", [T, 2 * KVW])


def build(nc, A, out, phases=None):
    with ExitStack() as stack:
        C = Shared(nc, stack)
        todo = [lambda: constants_phase(nc, C), lambda: pool_phase(nc, A, C), lambda: route_phase(nc, C, 0),
                lambda: experts_phase(nc, A, C, 0), lambda: combine_phase(nc, A, C, 0, out),
                lambda: attention_phase(nc, A, C), lambda: route_phase(nc, C, 1),
                lambda: experts_phase(nc, A, C, 1), lambda: combine_phase(nc, A, C, 1, out)]
        for n, phase in enumerate(todo):
            if phases is None or n in phases:
                phase()


_INS = ['x', 'p', 'positions', 'g_mix', 'g_ffn', 'pool_w', 'pool_scale', 'g_kv', 'w_k', 'w_v', 'w_q', 'w_o', 'sinks',
        'w_group_router', 'b_group_router', 'w_expert_router', 'b_expert_router',
        'w_exp_gate', 'w_exp_up', 'w_exp_down', 'g_ple', 'w_ple_gate', 'w_ple_up', 'g_final']


def kernel(**inputs):
    import concourse.bacc as bacc
    from concourse.bass_utils import run_bass_kernel_spmd

    nc = bacc.Bacc("TRN2", target_bir_lowering=False, num_devices=1)
    arrays, A = {}, {}
    for name in _INS:
        arrays[f"in_{name}"] = a = np.ascontiguousarray(inputs[name])
        A[name] = nc.dram_tensor(f"in_{name}", a.shape, mybir.dt.from_np(a.dtype), kind="ExternalInput").ap()
    out = nc.dram_tensor("out", [1, T, D], F32, kind="ExternalOutput").ap()
    build(nc, A, out)
    r = run_bass_kernel_spmd(nc, [arrays], core_ids=[0])
    return r.results[0]["out"]
```

```python
from contextlib import ExitStack

import numpy as np

import concourse.bass as bass
from concourse import mybir

F32 = mybir.dt.float32
BF16 = mybir.dt.bfloat16
I32 = mybir.dt.int32
U32 = mybir.dt.uint32
ALU = mybir.AluOpType
ACT = mybir.ActivationFunctionType
AX_X = mybir.AxisListType.X

P = 128
D = 1024
T = 4096
NT = T // P
KD = D // P
WINDOWS = (2, 4, 8, 16)
POOL_GROUP = D // len(WINDOWS)
TAIL = max(WINDOWS)
HEAD = 64
NQ = 16
NKV = 4
KVW = NKV * HEAD
NGRP = 4
EPG = 8
NE = NGRP * EPG
NLOG = NGRP + NE
F = 512
KF = F // P
PLE = 256
KPLE = PLE // P
EPS = 1e-6
NEG = -1.0e30
MAX_TILES = 2 * NT + NE
WCHUNK = 2048
NCHUNK = 3 * D * F // P // WCHUNK
POOL_CHUNKS = 3
INV_FREQ = (np.float32(10000.0) ** (-np.arange(0, HEAD, 2, dtype=np.float32) / np.float32(HEAD))).astype(np.float32)


def wait(eng, sem, value):
    if isinstance(value, int) and value <= 0:
        return
    eng.wait_ge(sem, value)


def done(t, u, ring=2):
    return 16 * ((t - u) // ring + 1) if isinstance(t, int) else t * (16 // ring) + (16 - 16 // ring * u)


class Mem:

    def __init__(self, nc, tag, stack):
        self.nc, self.tag, self.stack = nc, tag, stack
        stack.enter_context(nc.cleanup_on_exit())

    def sb(self, name, shape, dt=F32):
        return self.stack.enter_context(self.nc.sbuf_tensor(f"{self.tag}_{name}", shape, dt))

    def ps(self, name, shape, dt=F32):
        return self.stack.enter_context(self.nc.psum_tensor(f"{self.tag}_ps_{name}", shape, dt))

    def sem(self, name):
        return self.nc.alloc_semaphore(f"{self.tag}_{name}")

    def sems(self, names):
        return [self.sem(n) for n in names.split()]


def row(vec):
    n = vec.shape[0]
    return vec.rearrange("(o n) -> o n", o=1).to_broadcast([P, n])


def mm3(pe, out, lhs_hi, lhs_lo, rhs_hi, rhs_lo, first, last):
    pe.matmul(out, lhs_hi, rhs_hi, start=first, stop=False)
    pe.matmul(out, lhs_hi, rhs_lo, start=False, stop=False)
    return pe.matmul(out, lhs_lo, rhs_hi, start=False, stop=last)


def constants_phase(nc, C):
    with ExitStack() as stack:
        m = Mem(nc, "cst", stack)
        keep = m.sb("keep", [P, 4, P])
        count = m.sb("count", [P, P])
        inv_count = m.sb("inv_count", [P, 4, P])
        band_first = m.sb("band_first", [P, len(WINDOWS), P])
        band_prev = m.sb("band_prev", [P, len(WINDOWS), TAIL])
        filled, masked, band_ready = m.sems("filled masked band_ready")
        block = stack.enter_context(nc.Block())

        @block.gpsimd
        def _(pool):
            pool.memset(C.ident[:], 0.0).then_inc(filled, 1)
            pool.memset(C.before[:], 1.0).then_inc(filled, 1)
            pool.memset(C.ones[:], 1.0).then_inc(filled, 1)
            pool.memset(keep[:], 1.0).then_inc(filled, 1)
            for g, w in enumerate(WINDOWS):
                pool.memset(band_prev[:, g, :], 1.0 / w).then_inc(filled, 1)
            pool.memset(C.minus_half[:], -0.5).then_inc(filled, 1)
            pool.memset(C.mask_first[:, 0:P], NEG).then_inc(filled, 1)
            pool.memset(C.mask_first[:, P:2 * P], 0.0).then_inc(filled, 1)
            pool.memset(C.mask[:], 0.0).then_inc(filled, 1)
            pool.wait_ge(filled, 12)
            pool.affine_select(out=C.ident[:], in_=C.ident[:], compare_op=ALU.not_equal, fill=1.0, base=0,
                               pattern=[[-1, P]], channel_multiplier=1).then_inc(masked, 1)
            pool.affine_select(out=C.before[:], in_=C.before[:], compare_op=ALU.is_ge, fill=0.0, base=-1,
                               pattern=[[1, P]], channel_multiplier=-1).then_inc(masked, 1)
            pool.affine_select(out=keep[:], in_=keep[:], compare_op=ALU.is_ge, fill=0.0, base=0,
                               pattern=[[0, 4], [1, P]], channel_multiplier=-1).then_inc(masked, 1)
            pool.affine_select(out=C.mask[:, P:2 * P], in_=C.mask[:, P:2 * P], compare_op=ALU.is_ge, fill=NEG,
                               base=0, pattern=[[-1, P]], channel_multiplier=1).then_inc(masked, 1)
            pool.affine_select(out=C.mask[:, 0:P], in_=C.mask[:, 0:P], compare_op=ALU.is_ge, fill=NEG,
                               base=-1, pattern=[[1, P]], channel_multiplier=-1).then_inc(masked, 1)
            pool.affine_select(out=C.mask_first[:, P:2 * P], in_=C.mask_first[:, P:2 * P], compare_op=ALU.is_ge,
                               fill=NEG, base=0, pattern=[[-1, P]], channel_multiplier=1).then_inc(masked, 1)
            for g, w in enumerate(WINDOWS):
                pool.affine_select(out=band_prev[:, g, :], in_=band_prev[:, g, :], compare_op=ALU.is_ge,
                                   fill=0.0, base=w - 1 - P, pattern=[[-1, TAIL]],
                                   channel_multiplier=1).then_inc(masked, 1)
            pool.wait_ge(masked, 10)
            for g, w in enumerate(WINDOWS):
                pool.affine_select(out=keep[:, g, :], in_=keep[:, g, :], compare_op=ALU.is_ge, fill=0.0,
                                   base=w - 1, pattern=[[-1, P]], channel_multiplier=1).then_inc(masked, 1)
            pool.iota(count[:], pattern=[[1, P]], base=1, channel_multiplier=0,
                      allow_small_or_imprecise_dtypes=True).then_inc(masked, 1)
            pool.iota(C.iota[:], pattern=[[1, P]], base=0, channel_multiplier=0,
                      allow_small_or_imprecise_dtypes=True).then_inc(masked, 1)
            pool.iota(C.lane[:], pattern=[[0, 1]], base=0, channel_multiplier=1,
                      allow_small_or_imprecise_dtypes=True).then_inc(masked, 1)

        @block.vector
        def _(dve):
            dve.wait_ge(masked, 17)
            dve.tensor_copy(C.ident_bf[:], C.ident[:]).then_inc(band_ready, 1)
            for g, w in enumerate(WINDOWS):
                dve.tensor_scalar(inv_count[:, g, :], count[:], float(w), None, ALU.min).then_inc(band_ready, 1)
            dve.wait_ge(band_ready, 5)
            dve.reciprocal(inv_count[:], inv_count[:]).then_inc(band_ready, 1)
            dve.wait_ge(band_ready, 6)
            dve.tensor_tensor(inv_count[:], inv_count[:], keep[:], ALU.mult).then_inc(band_ready, 1)
            dve.wait_ge(band_ready, 7)
            for g, w in enumerate(WINDOWS):
                dve.scalar_tensor_tensor(out=C.band[:, g, :], in0=keep[:, g, :], scalar=1.0 / w, in1=C.ident[:],
                                         op0=ALU.mult, op1=ALU.subtract).then_inc(band_ready, 1)
                dve.tensor_tensor(band_first[:, g, :], inv_count[:, g, :], C.ident[:],
                                  ALU.subtract).then_inc(band_ready, 1)
            dve.tensor_copy(C.band_prev[:], band_prev[:])
            dve.wait_ge(band_ready, 15)
            dve.tensor_copy(C.band_first[:, 0], band_first[:]).then_inc(band_ready, 1)
            dve.wait_ge(band_ready, 16)
            dve.tensor_tensor(C.band_first[:, 1], band_first[:], C.band_first[:, 0], ALU.subtract)


def load_router(nc, sp, A, m_wr, m_bias, layer, loaded):
    with nc.allow_non_contiguous_dma(reason="router columns, once"):
        sp.dma_start(m_wr[:, :, 0:NGRP],
                     A["w_group_router"][layer].rearrange("(k p) n -> p k n", p=P)).then_inc(loaded, 16)
        sp.dma_start(m_wr[:, :, NGRP:NLOG],
                     A["w_expert_router"][layer].rearrange("(k p) n -> p k n", p=P)).then_inc(loaded, 16)
        sp.dma_start(m_bias[:, 0:NGRP], row(A["b_group_router"][layer])).then_inc(loaded, 16)
        sp.dma_start(m_bias[:, NGRP:NLOG], row(A["b_expert_router"][layer])).then_inc(loaded, 16)


def pool_phase(nc, A, C):
    RING = 4
    with ExitStack() as stack:
        m = Mem(nc, "mix", stack)
        wpool = m.sb("wpool", [P, KD, POOL_GROUP])
        scale_row = m.sb("scale_row", [P, D])
        g_ffn = m.sb("g_ffn", [P, D])
        g_mix = m.sb("g_mix", [P, KD])
        w_router = m.sb("w_router", [P, KD, NLOG])
        bias = m.sb("bias", [P, NLOG])
        x = [m.sb(f"x{i}", [P, D]) for i in range(RING)]
        xn = [m.sb(f"xn{i}", [P, 2, D], BF16) for i in range(RING)]
        junk = m.sb("junk", [P, D])
        junk_h = m.sb("junk_h", [P, D])
        pooled = m.sb("pooled", [P, KD, P])
        h1 = [m.sb(f"h1_{u}", [P, D]) for u in (0, 1)]
        hn = m.sb("hn", [P, D])
        hnT = m.sb("hnT", [P, KD, P])
        hrow = [m.sb(f"hrow{u}", [P, 2 * D], BF16) for u in (0, 1)]
        ssx, msx, rsx = (m.sb(n, [P, RING]) for n in ("ssx", "msx", "rsx"))
        ssh, msh, rsh = (m.sb(n, [P, 1]) for n in ("ssh", "msh", "rsh"))
        zeros = m.sb("zeros", [P, D])
        ps_pool = m.ps("pool", [P, KD, P])
        ps_mix = m.ps("mix", [P, D])
        ps_T = m.ps("T", [P, KD, P])
        ps_log = m.ps("log", [P, 512])
        loaded, w_ready = m.sems("loaded w_ready")
        x_loaded = [m.sem(f"x_loaded{i}") for i in range(RING)]
        h1_stored, row_stored = ([m.sem(f"{n}{u}") for u in (0, 1)] for n in ("h1_st", "row_st"))
        ssx_done, msx_done, rsx_done, xh_done, xl_done, pool_done, pooled_done, mix_done, h1_done = m.sems(
            "ssx_done msx_done rsx_done xh_done xl_done pool_done pooled_done mix_done h1_done")
        ssh_done, msh_done, rsh_done, hn_done, hi_done, lo_done, T_done, hnT_done, log_done, logits_done = m.sems(
            "ssh_done msh_done rsh_done hn_done hi_done lo_done T_done hnT_done log_done logits_done")
        zeros_done, spare_filled = m.sems("zeros_done spare_filled")
        x_t = A["x"].rearrange("b (t p) d -> (b t) p d", p=P)
        h1_t = C.h_mid.rearrange("(t p) d -> t p d", p=P)
        row_t = C.hn_rows.rearrange("(t p) d -> t p d", p=P)
        spare_t = C.y_rows.rearrange("(t p) d -> t p d", p=P)
        block = stack.enter_context(nc.Block())

        def steps(eng, step):
            for s in range(-2, RING):
                step(s, s % RING)
            with eng.Fori(1, NT // RING - 1) as i:
                for r in range(RING):
                    step(RING * i + r, r)
            for s in range(NT - RING, NT + 2):
                step(s, s % RING)

        def has(t):
            return not isinstance(t, int) or 0 <= t < NT

        @block.sync
        def _(sp):
            for t in (0, 1):
                sp.dma_start(x[t][:], x_t[t]).then_inc(x_loaded[t], 16)
            sp.dma_start(wpool[:], A["pool_w"][0].rearrange("g (k p) e -> p (g k) e", p=P)).then_inc(loaded, 16)
            sp.dma_start(scale_row[:], row(A["pool_scale"][0])).then_inc(loaded, 16)
            sp.dma_start(g_ffn[:], row(A["g_ffn"][0])).then_inc(loaded, 16)
            with nc.allow_non_contiguous_dma(reason="one gain per partition, once"):
                sp.dma_start(g_mix[:], A["g_mix"][0].rearrange("(k p) -> p k", p=P)).then_inc(loaded, 16)
            load_router(nc, sp, A, w_router, bias, 0, loaded)
            sp.dma_start(x[2][:], x_t[2]).then_inc(x_loaded[2], 16)
            sp.wait_ge(zeros_done, 1)

            def step(s, r):
                if has(s) and has(s + 3):
                    wait(sp, h1_done, s)
                    sp.dma_start(x[(r + 3) % RING][:], x_t[s + 3]).then_inc(x_loaded[(r + 3) % RING], 16)
                if has(s - 1):
                    u = (r - 1) % 2
                    sp.wait_ge(h1_done, s)
                    sp.dma_start(h1_t[s - 1], h1[u][:]).then_inc(h1_stored[u], 16)
                    sp.dma_start(spare_t[s - 1 + (MAX_TILES + 1 - NT)], zeros[:]).then_inc(spare_filled, 16)
                    sp.wait_ge(lo_done, s)
                    sp.dma_start(row_t[s - 1], hrow[u][:]).then_inc(row_stored[u], 16)

            steps(sp, step)
            for u in (0, 1):
                sp.wait_ge(h1_stored[u], 8 * NT)
                sp.wait_ge(row_stored[u], 8 * NT)
            sp.wait_ge(spare_filled, 16 * NT)

        @block.gpsimd
        def _(pool):
            pool.memset(zeros[:], 0.0).then_inc(zeros_done, 1)

            def step(s, r):
                if has(s - 1):
                    pool.wait_ge(msh_done, s)
                    wait(pool, hn_done, s - 1)
                    pool.tensor_tensor(rsh[:], msh[:], C.minus_half[:], ALU.pow).then_inc(rsh_done, 1)
                if has(s + 2):
                    i = (r + 2) % RING
                    pool.wait_ge(msx_done, s + 3)
                    wait(pool, xl_done, s - 1)
                    pool.tensor_tensor(rsx[:, i:i + 1], msx[:, i:i + 1], C.minus_half[:], ALU.pow).then_inc(rsx_done, 1)

            steps(pool, step)

        @block.scalar
        def _(act):
            def step(s, r):
                if has(s - 2):
                    act.wait_ge(T_done, s - 1)
                    wait(act, log_done, s - 2)
                    act.activation(hnT[:], ps_T[:], ACT.Copy).then_inc(hnT_done, 1)
                if has(s):
                    act.wait_ge(pool_done, s + 1)
                    wait(act, mix_done, s)
                    act.activation(pooled[:], ps_pool[:], ACT.Copy).then_inc(pooled_done, 1)
                if has(s - 1):
                    act.wait_ge(h1_done, s)
                    wait(act, ssh_done, s - 1)
                    act.activation(junk_h[:], h1[(r - 1) % 2][:], ACT.Square, accum_out=ssh[:]).then_inc(ssh_done, 1)
                if has(s + 1):
                    i = (r + 1) % RING
                    act.wait_ge(rsx_done, s + 2)
                    wait(act, pool_done, s - 1)
                    act.activation(xn[i][:, 0, :], x[i][:], ACT.Copy, scale=rsx[:, i:i + 1]).then_inc(xh_done, 1)
                if has(s - 1):
                    u = (r - 1) % 2
                    act.wait_ge(hn_done, s)
                    wait(act, row_stored[u], done(s - 3, u) if has(s - 3) else 0)
                    act.activation(hrow[u][:, 0:D], hn[:], ACT.Copy).then_inc(hi_done, 1)
                if has(s + 2):
                    i = (r + 2) % RING
                    act.wait_ge(x_loaded[i], done(s + 2, i, RING))
                    wait(act, ssx_done, s + 2)
                    act.activation(junk[:], x[i][:], ACT.Square, accum_out=ssx[:, i:i + 1]).then_inc(ssx_done, 1)

            steps(act, step)

        @block.vector
        def _(dve):
            def weights():
                dve.wait_ge(loaded, 16 * 8)
                for k in range(KD):
                    g = k * P // POOL_GROUP
                    dve.scalar_tensor_tensor(out=wpool[:, k, :], in0=wpool[:, k, :], scalar=g_mix[:, k:k + 1],
                                             in1=scale_row[:, g * POOL_GROUP:(g + 1) * POOL_GROUP],
                                             op0=ALU.mult, op1=ALU.mult).then_inc(w_ready, 1)

            def step(s, r):
                if isinstance(s, int) and s == 0:
                    weights()
                if has(s - 1):
                    u = (r - 1) % 2
                    dve.wait_ge(mix_done, s)
                    wait(dve, h1_stored[u], done(s - 3, u) if has(s - 3) else 0)
                    dve.tensor_tensor(h1[u][:], ps_mix[:], x[(r - 1) % RING][:], ALU.add).then_inc(h1_done, 1)
                    dve.wait_ge(ssh_done, s)
                    dve.tensor_scalar(msh[:], ssh[:], 1.0 / D, EPS, ALU.mult, ALU.add).then_inc(msh_done, 1)
                if has(s - 2):
                    at = slice(s - 2, s - 1) if isinstance(s, int) else bass.ds(s - 2, 1)
                    dve.wait_ge(log_done, s - 1)
                    dve.tensor_tensor(C.logits[:, at, :].rearrange("p a b -> p (a b)"), ps_log[:, 0:NLOG], bias[:],
                                      ALU.add).then_inc(logits_done, 1)
                if has(s - 1):
                    dve.wait_ge(rsh_done, s)
                    wait(dve, T_done, s - 1)
                    wait(dve, lo_done, s - 1)
                    dve.scalar_tensor_tensor(out=hn[:], in0=h1[u][:], scalar=rsh[:, 0:1], in1=g_ffn[:],
                                             op0=ALU.mult, op1=ALU.mult).then_inc(hn_done, 1)
                if has(s + 1):
                    i = (r + 1) % RING
                    dve.wait_ge(xh_done, s + 2)
                    dve.scalar_tensor_tensor(out=xn[i][:, 1, :], in0=x[i][:], scalar=rsx[:, i:i + 1], in1=xn[i][:, 0, :],
                                             op0=ALU.mult, op1=ALU.subtract).then_inc(xl_done, 1)
                if has(s - 1):
                    dve.wait_ge(hi_done, s)
                    dve.wait_ge(hn_done, s)
                    dve.tensor_tensor(hrow[u][:, D:2 * D], hn[:], hrow[u][:, 0:D], ALU.subtract).then_inc(lo_done, 1)
                if has(s + 2):
                    i = (r + 2) % RING
                    dve.wait_ge(ssx_done, s + 3)
                    dve.tensor_scalar(msx[:, i:i + 1], ssx[:, i:i + 1], 1.0 / D, EPS, ALU.mult, ALU.add).then_inc(msx_done, 1)

            steps(dve, step)

        @block.tensor
        def _(pe):
            def step(s, r):
                if has(s):
                    pe.wait_ge(xl_done, s + 1)
                    wait(pe, pooled_done, s)
                    first = isinstance(s, int) and s == 0
                    here, before = xn[r], xn[(r - 1) % RING]
                    for k in range(KD):
                        g = k * P // POOL_GROUP
                        c = slice(k * P, (k + 1) * P)
                        if first:
                            mm = mm3(pe, ps_pool[:, k, :], here[:, 0, c], here[:, 1, c], C.band_first[:, 0, g, :],
                                     C.band_first[:, 1, g, :], True, True)
                            continue
                        for part in (0, 1):
                            pe.matmul(ps_pool[:, k, :], here[:, part, c], C.band[:, g, :], start=part == 0, stop=False)
                        for part in (0, 1):
                            mm = pe.matmul(ps_pool[:, k, 0:TAIL], before[:, part, c], C.band_prev[:, g, :],
                                           start=False, stop=part == 1)
                    mm.then_inc(pool_done, 1)
                if has(s - 2):
                    pe.wait_ge(hnT_done, s - 1)
                    wait(pe, logits_done, s - 2)
                    for k in range(KD):
                        mm = pe.matmul(ps_log[:, 0:NLOG], hnT[:, k, :], w_router[:, k, :], start=k == 0, stop=k == KD - 1)
                    mm.then_inc(log_done, 1)
                if has(s):
                    if first:
                        pe.wait_ge(w_ready, KD)
                    pe.wait_ge(pooled_done, s + 1)
                    wait(pe, h1_done, s)
                    for k in range(KD):
                        g, kk = divmod(k, POOL_GROUP // P)
                        mm = pe.matmul(ps_mix[:, g * POOL_GROUP:(g + 1) * POOL_GROUP], pooled[:, k, :], wpool[:, k, :],
                                       start=kk == 0, stop=kk == POOL_GROUP // P - 1)
                    mm.then_inc(mix_done, 1)
                if has(s - 1):
                    pe.wait_ge(hn_done, s)
                    wait(pe, hnT_done, s - 1)
                    for k in range(KD):
                        mm = pe.transpose(ps_T[:, k, :], hn[:, k * P:(k + 1) * P], C.ident[:])
                    mm.then_inc(T_done, 1)

            steps(pe, step)


def route_phase(nc, C, layer):
    with ExitStack() as stack:
        m = Mem(nc, f"rt{layer}", stack)
        gl = m.sb("gl", [P, NT, 8])
        gmax = m.sb("gmax", [P, NT, 8])
        gidx = m.sb("gidx", [P, NT, 8], U32)
        gsel = m.sb("gsel", [P, NT])
        pen = m.sb("pen", [P, NT, NGRP])
        ex = m.sb("ex", [P, NT, NGRP])
        esum = m.sb("esum", [P, NT])
        el = m.sb("el", [P, NT, NE])
        emax = m.sb("emax", [P, NT, 8])
        eidx = m.sb("eidx", [P, NT, 8], U32)
        esel = m.sb("esel", [P, 2, NT])
        ediff = m.sb("ediff", [P, NT])
        den = m.sb("den", [P, NT])
        one_hot = [m.sb(f"one_hot{c}", [P, NT, NE]) for c in (0, 1)]
        both = m.sb("both", [P, NT, NE])
        total = m.sb("total", [P, NT, NE])
        scan = [m.sb(f"scan{c}", [P, NT, NE]) for c in (0, 1)]
        tiles_i = m.sb("tiles_i", [P, NE], I32)
        tiles_f = [m.sb(f"tiles_f{c}", [P, NE]) for c in (0, 1, 2)]
        ends_f = m.sb("ends_f", [P, NE + 1])
        slot_f = m.sb("slot_f", [P, 2, NT])
        slot_i = m.sb("slot_i", [P, 2, NT], I32)
        lo_i = m.sb("lo_i", [P, 2 * NT], I32)
        hi_i = m.sb("hi_i", [P, 2 * NT], I32)
        lo_f = m.sb("lo_f", [P, 2 * NT])
        hi_f = m.sb("hi_f", [P, 2 * NT])
        B = 8
        is_lo = [m.sb(f"is_lo{c}", [P, B, P], BF16) for c in (0, 1)]
        is_hi = [m.sb(f"is_hi{c}", [P, B, MAX_TILES], BF16) for c in (0, 1)]
        token = [m.sb(f"token{c}", [P, B, 2, MAX_TILES], BF16) for c in (0, 1)]
        part = m.sb("part", [P, 2, MAX_TILES])
        ps_before = m.ps("before", [P, NT, NE])
        ps_total = m.ps("total", [P, NT, NE])
        ps_token = m.ps("token", [P, 512])
        s, e_in, e_out, ranked, summed, hot_done, token_done = m.sems(
            "dve_step exp_in exp_out ranked summed hot_done token_done")
        block = stack.enter_context(nc.Block())

        @block.scalar
        def _(act):
            act.wait_ge(e_in, 1)
            act.activation(ex[:], ex[:], ACT.Exp).then_inc(e_out, 1)
            act.wait_ge(e_in, 2)
            act.activation(ediff[:], ediff[:], ACT.Exp).then_inc(e_out, 1)

        @block.tensor
        def _(pe):
            pe.wait_ge(ranked, 1)
            for h in (0, 1):
                tt = slice(h * NT // 2, (h + 1) * NT // 2)
                pe.matmul(ps_before[:, tt, :], C.before[:], both[:, tt, :], start=True, stop=True)
                mm = pe.matmul(ps_total[:, tt, :], C.ones[:], both[:, tt, :], start=True, stop=True)
            mm.then_inc(summed, 1)
            for b in range(2 * NT // B):
                pe.wait_ge(hot_done, b + 1)
                for j in range(B):
                    mm = pe.matmul(ps_token[:, 0:2 * MAX_TILES], is_lo[b % 2][:, j, :],
                                   token[b % 2][:, j, :, :].rearrange("p a b -> p (a b)"),
                                   start=b == 0 and j == 0, stop=b == 2 * NT // B - 1 and j == B - 1)
                mm.then_inc(token_done, 1)

        @block.vector
        def _(dve):
            n = [0]

            def link(ins):
                n[0] += 1
                ins.then_inc(s, 1)
                dve.wait_ge(s, n[0])

            L = C.logits
            link(dve.memset(gl[:], -3.0e38))
            link(dve.tensor_copy(gl[:, :, 0:NGRP], L[:, :, 0:NGRP]))
            for t in range(NT):
                dve.max(gmax[:, t, :], gl[:, t, :])
            link(dve.memset(C.zero[:], 0.0))
            for t in range(NT):
                dve.max_index(gidx[:, t, :], gmax[:, t, :], gl[:, t, :])
            link(dve.memset(C.zero[:], 0.0))
            dve.tensor_tensor(ex[:], gl[:, :, 0:NGRP], gmax[:, :, 0:1].to_broadcast([P, NT, NGRP]),
                              ALU.subtract).then_inc(e_in, 1)
            link(dve.tensor_copy(gsel[:], gidx[:, :, 0]))
            link(dve.tensor_tensor(pen[:], C.iota[:, 0:NGRP].unsqueeze(1).to_broadcast([P, NT, NGRP]),
                                   gsel[:].unsqueeze(2).to_broadcast([P, NT, NGRP]), ALU.is_equal))
            link(dve.tensor_scalar(pen[:], pen[:], -NEG, NEG, ALU.mult, ALU.add))
            link(dve.tensor_tensor(el[:].rearrange("p t (g e) -> p t g e", g=NGRP),
                                   L[:, :, NGRP:NLOG].rearrange("p t (g e) -> p t g e", g=NGRP),
                                   pen[:].unsqueeze(3).to_broadcast([P, NT, NGRP, EPG]), ALU.add))
            for t in range(NT):
                dve.max(emax[:, t, :], el[:, t, :])
            link(dve.memset(C.zero[:], 0.0))
            for t in range(NT):
                dve.max_index(eidx[:, t, :], emax[:, t, :], el[:, t, :])
            link(dve.memset(C.zero[:], 0.0))
            dve.tensor_tensor(ediff[:], emax[:, :, 1], emax[:, :, 0], ALU.subtract).then_inc(e_in, 1)
            for c in (0, 1):
                link(dve.tensor_copy(esel[:, c, :], eidx[:, :, c]))
                link(dve.tensor_tensor(one_hot[c][:], C.iota[:, 0:NE].unsqueeze(1).to_broadcast([P, NT, NE]),
                                       esel[:, c, :].unsqueeze(2).to_broadcast([P, NT, NE]), ALU.is_equal))
            dve.tensor_tensor(both[:], one_hot[0][:], one_hot[1][:], ALU.add).then_inc(ranked, 1)
            dve.wait_ge(e_out, 1)
            link(dve.reduce_sum(esum[:], ex[:], axis=AX_X))
            dve.wait_ge(e_out, 2)
            link(dve.tensor_scalar(den[:], ediff[:], 1.0, None, ALU.add))
            link(dve.tensor_tensor(den[:], den[:], esum[:], ALU.mult))
            link(dve.reciprocal(C.gates[:, 0, :], den[:]))
            link(dve.tensor_tensor(C.gates[:, 1, :], C.gates[:, 0, :], ediff[:], ALU.mult))
            dve.wait_ge(summed, 1)
            dve.tensor_copy(total[:], ps_total[:])
            link(dve.tensor_copy(scan[0][:], ps_total[:]))
            a = 0
            step = 1
            while step < NT:
                dve.tensor_copy(scan[1 - a][:, 0:step, :], scan[a][:, 0:step, :])
                link(dve.tensor_tensor(scan[1 - a][:, step:NT, :], scan[a][:, step:NT, :], scan[a][:, 0:NT - step, :], ALU.add))
                a, step = 1 - a, 2 * step
            link(dve.tensor_copy(tiles_i[:], scan[a][:, NT - 1, :]))
            link(dve.tensor_scalar(tiles_f[2][:], scan[a][:, NT - 1, :], float(P - 1), None, ALU.add))
            link(dve.tensor_copy(tiles_i[:], tiles_f[2][:]))
            link(dve.tensor_scalar(tiles_i[:], tiles_i[:], 7, None, ALU.arith_shift_right))
            link(dve.tensor_copy(tiles_f[2][:], tiles_i[:]))
            link(dve.tensor_scalar(tiles_f[2][:], tiles_f[2][:], 1.0, None, ALU.max))
            link(dve.tensor_copy(tiles_f[0][:], tiles_f[2][:]))
            b, step = 0, 1
            while step < NE:
                dve.tensor_copy(tiles_f[1 - b][:, 0:step], tiles_f[b][:, 0:step])
                link(dve.tensor_tensor(tiles_f[1 - b][:, step:NE], tiles_f[b][:, step:NE], tiles_f[b][:, 0:NE - step], ALU.add))
                b, step = 1 - b, 2 * step
            link(dve.memset(ends_f[:, 0:1], 0.0))
            link(dve.tensor_copy(ends_f[:, 1:NE + 1], tiles_f[b][:]))
            link(dve.tensor_copy(C.ends[:], ends_f[0:1, :]))
            link(dve.tensor_tensor(scan[a][:], scan[a][:], total[:], ALU.subtract))
            link(dve.tensor_tensor(scan[a][:], scan[a][:], ps_before[:], ALU.add))
            link(dve.scalar_tensor_tensor(out=scan[a][:], in0=ends_f[:, 0:NE].unsqueeze(1).to_broadcast([P, NT, NE]),
                                          scalar=float(P), in1=scan[a][:], op0=ALU.mult, op1=ALU.add))
            for c in (0, 1):
                link(dve.tensor_tensor(scan[1 - a][:], scan[a][:], one_hot[c][:], ALU.mult))
                link(dve.reduce_sum(slot_f[:, c, :], scan[1 - a][:], axis=AX_X))
            link(dve.tensor_copy(slot_i[:], slot_f[:]))
            link(dve.tensor_scalar(slot_f[:], slot_f[:], float(P), None, ALU.add))
            link(dve.tensor_copy(C.slot_row[:], slot_f[:]))
            flat = slot_i[:].rearrange("p c t -> p (c t)")
            link(dve.tensor_scalar(lo_i[:], flat, P - 1, None, ALU.bitwise_and))
            link(dve.tensor_scalar(hi_i[:], flat, 7, None, ALU.arith_shift_right))
            link(dve.tensor_copy(lo_f[:], lo_i[:]))
            link(dve.tensor_copy(hi_f[:], hi_i[:]))
            for b8 in range(2 * NT // B):
                w = b8 % 2
                cols = slice(b8 * B, (b8 + 1) * B)
                wait(dve, token_done, b8 - 1)
                t0 = b8 * B % NT
                dve.tensor_tensor(is_lo[w][:], C.iota[:].unsqueeze(1).to_broadcast([P, B, P]),
                                  lo_f[:, cols].unsqueeze(2).to_broadcast([P, B, P]), ALU.is_equal)
                link(dve.tensor_tensor(is_hi[w][:], C.iota[:, 0:MAX_TILES].unsqueeze(1).to_broadcast([P, B, MAX_TILES]),
                                       hi_f[:, cols].unsqueeze(2).to_broadcast([P, B, MAX_TILES]), ALU.is_equal))
                dve.tensor_scalar(token[w][:, :, 0, :], is_hi[w][:], C.lane[:, 0:1], None, ALU.mult)
                link(dve.tensor_tensor(token[w][:, :, 1, :], is_hi[w][:],
                                       C.iota[:, t0:t0 + B].unsqueeze(2).to_broadcast([P, B, MAX_TILES]), ALU.mult))
                dve.sem_inc(hot_done, 1)
            dve.wait_ge(token_done, 2 * NT // B)
            link(dve.tensor_copy(part[:].rearrange("p a b -> p (a b)"), ps_token[:, 0:2 * MAX_TILES]))
            link(dve.scalar_tensor_tensor(out=part[:, 0, :], in0=part[:, 1, :], scalar=float(P), in1=part[:, 0, :],
                                          op0=ALU.mult, op1=ALU.add))
            dve.memset(C.slot_token[:, MAX_TILES:MAX_TILES + 1], 0)
            link(dve.tensor_copy(C.slot_token[:, 0:MAX_TILES], part[:, 0, :]))


def experts_phase(nc, A, C, layer):
    with ExitStack() as stack:
        m = Mem(nc, f"ex{layer}", stack)
        raw = m.sb("raw", [P, NCHUNK, WCHUNK])
        w_hi = [m.sb(f"w_hi{u}", [P, NCHUNK * WCHUNK], BF16) for u in (0, 1)]
        w_lo = [m.sb(f"w_lo{u}", [P, NCHUNK * WCHUNK], BF16) for u in (0, 1)]
        token = m.sb("token", [P, 1], I32)
        xrow = m.sb("xrow", [P, 2 * D], BF16)
        xT = m.sb("xT", [P, 2, KD, P], BF16)
        silu = m.sb("silu", [P, F])
        a32 = m.sb("a32", [P, F])
        a = m.sb("a", [P, 2, F], BF16)
        aT = m.sb("aT", [P, 2, KF, P], BF16)
        y = m.sb("y", [P, D])
        ps_gate = m.ps("gate", [P, F])
        ps_up = [m.ps(f"up{h}", [P, 512]) for h in (0, 1)]
        ps_xT = m.ps("xT", [P, 2, KD, P], BF16)
        turned = "p (h k n) -> p h k n"
        ps_aT = [m.ps("aT", [P, 2, KF // 2, P], BF16)[:],
                 ps_up[0][:, F // 2:512].bitcast(BF16).rearrange(turned, h=2, k=KF // 2)]
        ps_y = m.ps("y", [P, D])
        raw_loaded = [m.sem(f"raw_loaded{c}") for c in range(NCHUNK)]
        hi_done, pool_lo, dve_lo, token_done, token_seen, gathered, xT_mm, xT_done = m.sems(
            "hi_done pool_lo dve_lo token_done token_seen gathered xT_mm xT_done")
        gate_mm, silu_done, up_mm, a_mul, a_done = m.sems("gate_mm silu_done up_mm a_mul a_done")
        aT_mm, aT_done, down_mm, y_done, y_stored, last_stored = m.sems("aT_mm aT_done down_mm y_done y_stored last_stored")
        halves = "l e (h k p) n -> (l e h) p k n"
        src = [A[n].rearrange(halves, p=P, k=WCHUNK // w) for n, w in (("w_exp_gate", F), ("w_exp_up", F), ("w_exp_down", D))]
        y_t = C.y_rows.rearrange("(t p) d -> t p d", p=P)
        block = stack.enter_context(nc.Block())

        def bounds(eng, e):
            return (eng.value_load(C.ends[0:1, bass.ds(e, 1)], min_val=0, max_val=MAX_TILES - 2),
                    eng.value_load(C.ends[0:1, bass.ds(e + 1, 1)], min_val=1, max_val=MAX_TILES - 1))

        def wait_split(eng, e, c):
            if c < POOL_CHUNKS:
                eng.wait_ge(pool_lo, POOL_CHUNKS * e + c + 1)
            else:
                eng.wait_ge(dve_lo, (NCHUNK - POOL_CHUNKS) * e + c - POOL_CHUNKS + 1)

        def lo_part(eng, e, u, c, lo_done):
            eng.wait_ge(hi_done, NCHUNK * e + c + 1)
            w = slice(c * WCHUNK, (c + 1) * WCHUNK)
            eng.tensor_tensor(w_lo[u][:, w], raw[:, c, :], w_hi[u][:, w], ALU.subtract).then_inc(lo_done, 1)

        @block.sync
        def _(sp):
            def load(e, c):
                part, half = divmod(c, 2)
                ap = src[part][layer * 2 * NE + 2 * e + half]
                sp.dma_start(raw[:, c, :].rearrange("p (k n) -> p k n", k=ap.shape[1]), ap).then_inc(raw_loaded[c], 16)

            for c in range(NCHUNK):
                load(0, c)
            with sp.Fori(0, NE - 1) as e:
                for c in range(NCHUNK):
                    wait_split(sp, e, c)
                    load(e + 1, c)

        @block.scalar
        def _(act):
            def split(e, u):
                if not isinstance(e, int):
                    ends = act.value_load(C.ends[0:1, bass.ds(e - 1, 1)], min_val=1, max_val=MAX_TILES - 1)
                for c in range(NCHUNK):
                    act.wait_ge(raw_loaded[c], 16 * (e + 1))
                    if not isinstance(e, int):
                        act.wait_ge((gate_mm, up_mm, down_mm)[c // 2], ends * (1, 2, 2)[c // 2])
                    act.activation(w_hi[u][:, c * WCHUNK:(c + 1) * WCHUNK], raw[:, c, :], ACT.Copy).then_inc(hi_done, 1)

            def store(k, stored):
                act.wait_ge(y_done, 2 * k + 4)
                act.dma_start(y_t[k + 1], y[:]).then_inc(stored, 16)

            def tiles(e):
                first, end = bounds(act, e)
                with act.Fori(first, end) as k:
                    act.wait_ge(gate_mm, k + 1)
                    act.activation(silu[:], ps_gate[:], ACT.Silu).then_inc(silu_done, 1)
                    store(k - 1, y_stored)
                return end

            split(0, 0)
            split(1, 1)
            tiles(0)
            with act.Fori(0, NE // 2 - 1) as i:
                for u in (0, 1):
                    split(2 * i + u + 2, u)
                    tiles(2 * i + u + 1)
            end = tiles(NE - 1)
            store(end - 1, last_stored)
            act.wait_ge(last_stored, 16)

        @block.gpsimd
        def _(pool):
            def split(e, u):
                for c in range(POOL_CHUNKS):
                    lo_part(pool, e, u, c, pool_lo)

            def gather(k):
                at = slice(k, k + 1) if isinstance(k, int) else bass.ds(k, 1)
                pool.tensor_copy(token[:], C.slot_token[:, at]).then_inc(token_done, 1)
                pool.wait_ge(token_done, k + 1)
                pool.sem_inc(token_seen, 1)
                pool.indirect_dma_start(xrow[:], None, C.hn_rows, bass.IndirectOffsetOnAxis(ap=token[:, 0:1], axis=0)).then_inc(gathered, 16)

            def tiles(e):
                first, end = bounds(pool, e)
                with pool.Fori(first, end) as k:
                    pool.wait_ge(xT_mm, k + 2)
                    gather(k + 2)
                return end

            gather(0)
            pool.wait_ge(xT_mm, 1)
            gather(1)
            split(0, 0)
            split(1, 1)
            tiles(0)
            with pool.Fori(0, NE // 2 - 1) as i:
                for u in (0, 1):
                    split(2 * i + u + 2, u)
                    tiles(2 * i + u + 1)
            end = tiles(NE - 1)
            pool.wait_ge(gathered, end * 16 + 32)

        @block.vector
        def _(dve):
            def split(e, u):
                for c in range(POOL_CHUNKS, NCHUNK):
                    lo_part(dve, e, u, c, dve_lo)

            def take_x(k):
                dve.wait_ge(xT_mm, k + 1)
                dve.tensor_copy(xT[:], ps_xT[:]).then_inc(xT_done, 1)

            def tiles(e):
                first, end = bounds(dve, e)
                with dve.Fori(first, end) as k:
                    dve.wait_ge(silu_done, k + 1)
                    for h in (0, 1):
                        c = slice(h * F // 2, (h + 1) * F // 2)
                        dve.wait_ge(up_mm, 2 * k + h + 1)
                        dve.tensor_tensor(a[:, 0, c], silu[:, c], ps_up[h][:, 0:F // 2], ALU.mult)
                        dve.tensor_tensor(a32[:, c], silu[:, c], ps_up[h][:, 0:F // 2], ALU.mult).then_inc(a_mul, 1)
                        dve.wait_ge(a_mul, 2 * k + h + 1)
                        dve.tensor_tensor(a[:, 1, c], a32[:, c], a[:, 0, c], ALU.subtract).then_inc(a_done, 1)
                        j = slice(h * KF // 2, (h + 1) * KF // 2)
                        dve.wait_ge(aT_mm, 2 * k + h + 1)
                        dve.tensor_copy(aT[:, :, j, :], ps_aT[h]).then_inc(aT_done, 1)
                    take_x(k + 1)
                    dve.wait_ge(y_stored, 16 * k + 16)
                    for n in (0, 1):
                        dve.wait_ge(down_mm, 2 * k + n + 1)
                        c = slice(512 * n, 512 * n + 512)
                        dve.tensor_copy(y[:, c], ps_y[:, c]).then_inc(y_done, 1)

            dve.memset(y[:], 0.0).then_inc(y_done, 2)
            take_x(0)
            split(0, 0)
            split(1, 1)
            tiles(0)
            with dve.Fori(0, NE // 2 - 1) as i:
                for u in (0, 1):
                    split(2 * i + u + 2, u)
                    tiles(2 * i + u + 1)
            tiles(NE - 1)

        @block.tensor
        def _(pe):
            def turn_x(k):
                pe.wait_ge(gathered, 16 * k + 16)
                for h in (0, 1):
                    for j in range(KD):
                        mm = pe.transpose(ps_xT[:, h, j, :], xrow[:, h * D + j * P:h * D + (j + 1) * P], C.ident_bf[:])
                mm.then_inc(xT_mm, 1)

            def turn_a(k, h):
                pe.wait_ge(a_done, 2 * k + h + 1)
                for part in (0, 1):
                    for i in range(KF // 2):
                        j = h * KF // 2 + i
                        mm = pe.transpose(ps_aT[h][:, part, i, :], a[:, part, j * P:(j + 1) * P], C.ident_bf[:])
                mm.then_inc(aT_mm, 1)

            def into_f(ps, u, part, c, rows):
                for j in rows:
                    w = slice((part * KD + j) * F + c.start, (part * KD + j) * F + c.stop)
                    mm = mm3(pe, ps, xT[:, 0, j, :], xT[:, 1, j, :], w_hi[u][:, w], w_lo[u][:, w], j == 0, j == KD - 1)
                return mm

            def down(u, h, n):
                for j in range(h * KF // 2, (h + 1) * KF // 2):
                    w = slice(2 * KD * F + j * D + n * 512, 2 * KD * F + j * D + (n + 1) * 512)
                    mm = mm3(pe, ps_y[:, n * 512:(n + 1) * 512], aT[:, 0, j, :], aT[:, 1, j, :], w_hi[u][:, w],
                             w_lo[u][:, w], j == 0, j == KF - 1)
                return mm

            turn_x(0)

            def tiles(e, u):
                first, end = bounds(pe, e)
                with pe.Fori(first, end) as k:
                    pe.wait_ge(xT_done, k + 1)
                    turn_x(k + 1)
                    wait_split(pe, e, 1)
                    into_f(ps_gate[:], u, 0, slice(0, F), range(KD)).then_inc(gate_mm, 1)
                    wait_split(pe, e, 2)
                    wait_split(pe, e, 3)
                    into_f(ps_up[0][:, 0:F // 2], u, 1, slice(0, F // 2), range(KD)).then_inc(up_mm, 1)
                    into_f(ps_up[1][:, 0:F // 2], u, 1, slice(F // 2, F), range(KD - 2))
                    turn_a(k, 0)
                    into_f(ps_up[1][:, 0:F // 2], u, 1, slice(F // 2, F), range(KD - 2, KD)).then_inc(up_mm, 1)
                    wait_split(pe, e, NCHUNK - 1)
                    pe.wait_ge(y_done, 2 * k + 2)
                    pe.wait_ge(aT_done, 2 * k + 1)
                    down(u, 0, 0)
                    turn_a(k, 1)
                    down(u, 0, 1)
                    pe.wait_ge(aT_done, 2 * k + 2)
                    down(u, 1, 0).then_inc(down_mm, 1)
                    down(u, 1, 1).then_inc(down_mm, 1)

            with pe.Fori(0, NE // 2) as i:
                for u in (0, 1):
                    tiles(2 * i + u, u)


def split_weights(nc, C, tag, gains, jobs):
    depth = 4
    with ExitStack() as stack:
        m = Mem(nc, tag, stack)
        width = max(job[2].shape[1] for job in jobs)
        raw = [m.sb(f"raw{i}", [P, width]) for i in range(depth)]
        raw_loaded = [m.sem(f"raw_loaded{i}") for i in range(depth)]
        gain_loaded, gain_done, hi_done, lo_done = m.sems("gain_loaded gain_done hi_done lo_done")
        block = stack.enter_context(nc.Block())

        @block.sync
        def _(sp):
            with nc.allow_non_contiguous_dma(reason="one gain per partition, once"):
                for vec, _, gain in gains:
                    sp.dma_start(gain, vec.rearrange("(k p) -> p k", p=P)).then_inc(gain_loaded, 16)
            for n, (sources, _, hi, _) in enumerate(jobs):
                wait(sp, lo_done, n - depth + 1)
                for parts, rows in sources:
                    sp.dma_start(raw[n % depth][parts, 0:hi.shape[1]], rows).then_inc(raw_loaded[n % depth], 16)

        loads = [0] * depth
        landed = []
        for n, (sources, _, _, _) in enumerate(jobs):
            loads[n % depth] += 16 * len(sources)
            landed.append(loads[n % depth])

        @block.scalar
        def _(act):
            wait(act, gain_done, len(gains))
            for n, (_, gain, hi, _) in enumerate(jobs):
                act.wait_ge(raw_loaded[n % depth], landed[n])
                act.activation(hi, raw[n % depth][:, 0:hi.shape[1]], ACT.Copy,
                               scale=1.0 if gain is None else gain).then_inc(hi_done, 1)

        @block.vector
        def _(dve):
            wait(dve, gain_loaded, 16 * len(gains))
            for _, factor, gain in gains:
                dve.tensor_scalar(gain, gain, factor, None, ALU.mult).then_inc(gain_done, 1)
            wait(dve, gain_done, len(gains))
            for n, (_, gain, hi, lo) in enumerate(jobs):
                dve.wait_ge(hi_done, n + 1)
                src = raw[n % depth][:, 0:hi.shape[1]]
                dve.scalar_tensor_tensor(out=lo, in0=src, scalar=1.0 if gain is None else gain, in1=hi,
                                         op0=ALU.mult, op1=ALU.subtract).then_inc(lo_done, 1)


def rotary_tables(nc, A, C, cos, sin):
    magic = float(1.5 * 2 ** 23)
    two_pi = 2 * np.pi
    c1 = 6.28125
    c2 = float(np.floor((two_pi - c1) * 2 ** 21) / 2 ** 21)
    c3 = float(np.float32(two_pi - c1 - c2))
    edge = float(np.nextafter(np.float32(np.pi), np.float32(0)))
    if edge > np.pi:
        edge = float(np.nextafter(np.float32(edge), np.float32(0)))
    nf = HEAD // 2
    with ExitStack() as stack:
        m = Mem(nc, "rot", stack)
        pos_i = m.sb("pos_i", [P, NT], I32)
        pos = m.sb("pos", [P, NT])
        inv = m.sb("inv", [P, nf])
        turns = m.sb("turns", [P, NT, nf])
        loaded, step_done, ready = m.sems("loaded step_done ready")
        block = stack.enter_context(nc.Block())

        @block.sync
        def _(sp):
            with nc.allow_non_contiguous_dma(reason="one position per partition, once"):
                sp.dma_start(pos_i[:], A["positions"][0].rearrange("(t p) -> p t", p=P)).then_inc(loaded, 16)

        @block.scalar
        def _(act):
            act.wait_ge(ready, 1)
            act.activation(sin[:], sin[:], ACT.Sin)
            act.activation(cos[:], cos[:], ACT.Sin)

        @block.vector
        def _(dve):
            n = [0]

            def link(ins):
                n[0] += 1
                ins.then_inc(step_done, 1)
                dve.wait_ge(step_done, n[0])

            for j in range(nf):
                dve.memset(inv[:, j:j + 1], float(INV_FREQ[j]))
            dve.wait_ge(loaded, 16)
            link(dve.tensor_copy(pos[:], pos_i[:]))
            shape = [P, NT, nf]
            link(dve.tensor_tensor(sin[:], pos[:].unsqueeze(2).to_broadcast(shape), inv[:].unsqueeze(1).to_broadcast(shape), ALU.mult))
            link(dve.tensor_scalar(turns[:], sin[:], 1.0 / two_pi, magic, ALU.mult, ALU.add))
            link(dve.tensor_scalar(turns[:], turns[:], -magic, None, ALU.add))
            for c in (c1, c2, c3):
                link(dve.scalar_tensor_tensor(out=sin[:], in0=turns[:], scalar=-c, in1=sin[:], op0=ALU.mult, op1=ALU.add))
            link(dve.tensor_scalar(turns[:], sin[:], float(np.pi / 2), -two_pi, ALU.is_gt, ALU.mult))
            link(dve.scalar_tensor_tensor(out=cos[:], in0=sin[:], scalar=float(np.pi / 2), in1=turns[:], op0=ALU.add, op1=ALU.add))
            link(dve.tensor_scalar(cos[:], cos[:], edge, -edge, ALU.min, ALU.max))
            dve.tensor_scalar(sin[:], sin[:], edge, -edge, ALU.min, ALU.max).then_inc(ready, 1)


def combine_phase(nc, A, C, layer, out):
    qkv = layer == 0
    with ExitStack() as stack:
        m = Mem(nc, f"cb{layer}", stack)
        wg = m.sb("wg", [P, 2, KD, D], BF16)
        wu = m.sb("wu", [P, 2, KPLE, D], BF16)
        g_ple = m.sb("g_ple", [P, KD])
        gains = [(A["g_ple"][layer], 1.0, g_ple[:])]
        rows = lambda w, k: [(slice(0, P), w[k * P:(k + 1) * P, :])]
        jobs = [(rows(A["w_ple_gate"][layer], k), g_ple[:, k:k + 1], wg[:, 0, k, :], wg[:, 1, k, :]) for k in range(KD)]
        jobs += [(rows(A["w_ple_up"][layer], k), None, wu[:, 0, k, :], wu[:, 1, k, :]) for k in range(KPLE)]
        if qkv:
            wq = m.sb("wq", [P, 2, KD, D], BF16)
            wkv = m.sb("wkv", [P, 2, KD, 2 * KVW], BF16)
            g_q = m.sb("g_q", [P, KD])
            g_kv = m.sb("g_kv", [P, KD])
            cos = m.sb("cos", [P, NT, HEAD // 2])
            sin = m.sb("sin", [P, NT, HEAD // 2])
            gains += [(A["g_mix"][1], HEAD ** -0.5, g_q[:]), (A["g_kv"], 1.0, g_kv[:])]
            jobs += [(rows(A["w_q"][0], k), g_q[:, k:k + 1], wq[:, 0, k, :], wq[:, 1, k, :]) for k in range(KD)]
            for w, at in (("w_k", 0), ("w_v", KVW)):
                jobs += [(rows(A[w], k), g_kv[:, k:k + 1], wkv[:, 0, k, at:at + KVW], wkv[:, 1, k, at:at + KVW])
                         for k in range(KD)]
            rotary_tables(nc, A, C, cos, sin)
        split_weights(nc, C, f"cw{layer}", gains, jobs)

        g_final = None if qkv else m.sb("g_final", [P, D])
        slot = [m.sb(f"slot{u}", [P, 2], I32) for u in (0, 1)]
        hin = [m.sb(f"hin{u}", [P, D]) for u in (0, 1)]
        y0 = [m.sb(f"y0_{u}", [P, D]) for u in (0, 1)]
        y1 = [m.sb(f"y1_{u}", [P, D]) for u in (0, 1)]
        p_in = [m.sb(f"p_in{u}", [P, PLE]) for u in (0, 1)]
        h2 = [m.sb(f"h2_{u}", [P, D]) for u in (0, 1)]
        x = m.sb("x", [P, 2, D], BF16)
        ph = m.sb("ph", [P, 2, PLE], BF16)
        xT = [m.sb(f"xT{u}", [P, 2, KD, P], BF16) for u in (0, 1)]
        pT = [m.sb(f"pT{u}", [P, 2, KPLE, P], BF16) for u in (0, 1)]
        th = m.sb("th", [P, 2, 512])
        mid = m.sb("mid", [P, 2, 512])
        h3 = [m.sb(f"h3_{u}", [P, D]) for u in (0, 1)]
        junk = m.sb("junk", [P, D])
        ss2, ms2, rs2, ss3, ms3, rs3 = (m.sb(n, [P, 1]) for n in ("ss2", "ms2", "rs2", "ss3", "ms3", "rs3"))
        if qkv:
            x3 = m.sb("x3", [P, 2, D], BF16)
            x3T = m.sb("x3T", [P, 2, KD, P], BF16)
            ra = m.sb("ra", [P, 512])
            rb = m.sb("rb", [P, 512])
            q_out = m.sb("q_out", [P, D])
            kv_out = m.sb("kv_out", [P, 2 * KVW])
        else:
            o_out = [m.sb(f"o_out{u}", [P, D]) for u in (0, 1)]
        ps_x = m.ps("x", [P, 2, KD, P], BF16)
        ps_p = m.ps("p", [P, 2, KPLE, P], BF16)
        ps = [m.ps(f"b{i}", [P, 512]) for i in range(5)]
        ps_gate, ps_up = (ps[0], ps[2]), (ps[1], ps[3])
        ps_q, ps_kv = (ps[4], ps[0]), ps[1]
        g_loaded = m.sem("g_loaded")
        h_ld, p_ld, y_ld, h3_st, o_st = ([m.sem(f"{n}{u}") for u in (0, 1)] for n in ("h_ld", "p_ld", "y_ld", "h3_st", "o_st"))
        slot_done, slot_seen, part_done, h2_done, ss2_done, ms2_done, rs2_done = m.sems("slot_done slot_seen part_done h2_done ss2_done ms2_done rs2_done")
        xh_done, xl_done, ph_done, pl_done, x_mm, xT_done, pT_done = m.sems("xh_done xl_done ph_done pl_done x_mm xT_done pT_done")
        gate_mm, up_mm, th_done, mid_done, h3_done = m.sems("gate_mm up_mm th_done mid_done h3_done")
        ss3_done, ms3_done, rs3_done, x3h_done, x3l_done, x3_mm, x3T_done = m.sems("ss3_done ms3_done rs3_done x3h_done x3l_done x3_mm x3T_done")
        q_mm, kv_mm, v_done, rot_mul, rot_add, o_done, q_st = m.sems("q_mm kv_mm v_done rot_mul rot_add o_done q_st")
        h_t = C.h_mid.rearrange("(t p) d -> t p d", p=P)
        p_t = A["p"][layer].rearrange("b (t p) d -> (b t) p d", p=P)
        h3_t = C.h_out.rearrange("(t p) d -> t p d", p=P)
        q_t = C.q_rows.rearrange("(t p) d -> t p d", p=P)
        kv_t = C.kv_rows.rearrange("(t p) d -> t p d", p=P)
        out_t = out.rearrange("b (t p) d -> (b t) p d", p=P)
        block = stack.enter_context(nc.Block())

        def steps(eng, step):
            step(-2, 0, True, False, False, False)
            step(-1, 1, True, True, False, False)
            step(0, 0, True, True, True, False)
            step(1, 1, True, True, True, True)
            with eng.Fori(1, NT // 2 - 1) as i:
                step(2 * i, 0, True, True, True, True)
                step(2 * i + 1, 1, True, True, True, True)
            step(NT - 2, 0, False, True, True, True)
            step(NT - 1, 1, False, False, True, True)
            step(NT, 0, False, False, False, True)

        @block.sync
        def _(sp):
            if not qkv:
                sp.dma_start(g_final[:], row(A["g_final"])).then_inc(g_loaded, 16)

            def step(s, u, load, head, mid_, tail):
                if load:
                    t = s + 2
                    wait(sp, h2_done, t - 1)
                    sp.dma_start(hin[u][:], h_t[t]).then_inc(h_ld[u], 16)
                    wait(sp, pl_done, t - 1)
                    sp.dma_start(p_in[u][:], p_t[t]).then_inc(p_ld[u], 16)
                if mid_ and qkv:
                    sp.wait_ge(h3_done, 2 * s + 2)
                    sp.dma_start(h3_t[s], h3[u][:]).then_inc(h3_st[u], 16)
                if tail and qkv:
                    t = s - 1
                    sp.wait_ge(rot_add, 3 * t + 3)
                    sp.dma_start(q_t[t], q_out[:]).then_inc(q_st, 16)
                    sp.wait_ge(v_done, t + 1)
                    sp.dma_start(kv_t[t], kv_out[:]).then_inc(q_st, 16)
                if tail and not qkv:
                    t = s - 1
                    sp.wait_ge(o_done, t + 1)
                    sp.dma_start(out_t[t], o_out[1 - u][:]).then_inc(o_st[1 - u], 16)

            steps(sp, step)
            if qkv:
                sp.wait_ge(q_st, 32 * NT)
                for u in (0, 1):
                    sp.wait_ge(h3_st[u], 8 * NT)
            else:
                for u in (0, 1):
                    sp.wait_ge(o_st[u], 8 * NT)

        @block.gpsimd
        def _(pool):
            def step(s, u, load, head, mid_, tail):
                if load:
                    t = s + 2
                    wait(pool, h2_done, t - 1)
                    at = slice(t, t + 1) if isinstance(t, int) else bass.ds(t, 1)
                    pool.tensor_copy(slot[u][:], C.slot_row[:, :, at].rearrange("p c t -> p (c t)")).then_inc(slot_done, 1)
                    pool.wait_ge(slot_done, t + 1)
                    pool.sem_inc(slot_seen, 1)
                    for c, y in enumerate((y0, y1)):
                        pool.indirect_dma_start(y[u][:], None, C.y_rows,
                                                bass.IndirectOffsetOnAxis(ap=slot[u][:, c:c + 1], axis=0)).then_inc(y_ld[u], 16)
                if head:
                    pool.wait_ge(ms2_done, s + 2)
                    wait(pool, xl_done, s + 1)
                    pool.tensor_tensor(rs2[:], ms2[:], C.minus_half[:], ALU.pow).then_inc(rs2_done, 1)
                if mid_:
                    pool.wait_ge(ms3_done, s + 1)
                    wait(pool, x3l_done if qkv else o_done, s)
                    pool.tensor_tensor(rs3[:], ms3[:], C.minus_half[:], ALU.pow).then_inc(rs3_done, 1)

            steps(pool, step)

        @block.scalar
        def _(act):
            def step(s, u, load, head, mid_, tail):
                v = 1 - u
                if head:
                    t = s + 1
                    act.wait_ge(p_ld[v], done(t, v))
                    wait(act, x_mm, t)
                    act.activation(ph[:, 0, :], p_in[v][:], ACT.Copy).then_inc(ph_done, 1)
                    act.wait_ge(h2_done, t + 1)
                    wait(act, ss3_done, s)
                    wait(act, ss2_done, t)
                    act.activation(junk[:], h2[v][:], ACT.Square, accum_out=ss2[:]).then_inc(ss2_done, 1)
                if head:
                    t = s + 1
                    act.wait_ge(rs2_done, t + 1)
                    act.activation(x[:, 0, :], h2[v][:], ACT.Copy, scale=rs2[:, 0:1]).then_inc(xh_done, 1)
                if mid_:
                    for h in (0, 1):
                        act.wait_ge(gate_mm, 2 * s + h + 1)
                        wait(act, mid_done, 2 * s + h - 1)
                        act.activation(th[:, h, :], ps_gate[h][:], ACT.Tanh, scale=0.5).then_inc(th_done, 1)
                    act.wait_ge(h3_done, 2 * s + 2)
                    wait(act, ss3_done, s)
                    wait(act, ss2_done, s + 2 if head else 0)
                    act.activation(junk[:], h3[u][:], ACT.Square, accum_out=ss3[:]).then_inc(ss3_done, 1)
                    if qkv:
                        act.wait_ge(rs3_done, s + 1)
                        wait(act, x3_mm, s)
                        act.activation(x3[:, 0, :], h3[u][:], ACT.Copy, scale=rs3[:, 0:1]).then_inc(x3h_done, 1)

            steps(act, step)

        @block.vector
        def _(dve):
            if not qkv:
                dve.wait_ge(g_loaded, 16)

            def rotate(t, at, src, dst, heads, n, mm, mm_count, pairs):
                nf = HEAD // 2
                shape = [P, heads, nf]
                c = cos[:, at, :].rearrange("p a f -> p (a f)").unsqueeze(1)
                sn = sin[:, at, :].rearrange("p a f -> p (a f)").unsqueeze(1)
                w = heads * HEAD
                dve.wait_ge(mm, mm_count)
                wait(dve, rot_add, 3 * t + n)
                dve.tensor_tensor(ra[:, 0:w].rearrange("p (h f) -> p h f", f=nf), src.rearrange("p (h f) -> p h f", f=nf),
                                  c.to_broadcast([P, 2 * heads, nf]), ALU.mult)
                s4 = src.rearrange("p (h two f) -> p h two f", two=2, f=nf)
                a4 = ra[:, 0:w].rearrange("p (h two f) -> p h two f", two=2, f=nf)
                b4 = rb[:, 0:w].rearrange("p (h two f) -> p h two f", two=2, f=nf)
                dve.tensor_tensor(b4[:, :, 0, :], s4[:, :, 1, :], sn.to_broadcast(shape), ALU.mult)
                dve.tensor_tensor(b4[:, :, 1, :], s4[:, :, 0, :], sn.to_broadcast(shape), ALU.mult).then_inc(rot_mul, 1)
                dve.wait_ge(rot_mul, 3 * t + n + 1)
                for half, op in ((0, ALU.subtract), (1, ALU.add)):
                    i0, i1 = a4[:, :, half, :], b4[:, :, half, :]
                    o = dst.rearrange("p (h two f) -> p h two f", two=2, f=nf)[:, :, half, :]
                    if pairs:
                        i0 = i0.rearrange("p (s i) f -> p s i f", s=2)
                        i1 = i1.rearrange("p (s i) f -> p s i f", s=2)
                        o = o.rearrange("p (i s) f -> p s i f", s=2)
                    last = dve.tensor_tensor(o, i0, i1, op)
                last.then_inc(rot_add, 1)

            def step(s, u, load, head, mid_, tail):
                v = 1 - u
                if head:
                    t = s + 1
                    at = slice(t, t + 1) if isinstance(t, int) else bass.ds(t, 1)
                    dve.wait_ge(h_ld[v], done(t, v))
                    dve.wait_ge(y_ld[v], 2 * done(t, v))
                    dve.scalar_tensor_tensor(out=h2[v][:], in0=y0[v][:], scalar=C.gates[:, 0, at], in1=hin[v][:],
                                             op0=ALU.mult, op1=ALU.add).then_inc(part_done, 1)
                    dve.wait_ge(part_done, t + 1)
                    dve.scalar_tensor_tensor(out=h2[v][:], in0=y1[v][:], scalar=C.gates[:, 1, at], in1=h2[v][:],
                                             op0=ALU.mult, op1=ALU.add).then_inc(h2_done, 1)
                    dve.wait_ge(ph_done, t + 1)
                    dve.tensor_tensor(ph[:, 1, :], p_in[v][:], ph[:, 0, :], ALU.subtract).then_inc(pl_done, 1)
                    dve.wait_ge(ss2_done, t + 1)
                    dve.tensor_scalar(ms2[:], ss2[:], 1.0 / D, EPS, ALU.mult, ALU.add).then_inc(ms2_done, 1)
                if tail and qkv:
                    t = s - 1
                    dve.wait_ge(x3_mm, t + 1)
                    wait(dve, kv_mm, t)
                    dve.tensor_copy(x3T[:], ps_x[:]).then_inc(x3T_done, 1)
                if tail and not qkv:
                    t = s - 1
                    dve.wait_ge(rs3_done, t + 1)
                    wait(dve, o_st[v], done(t - 2, v) if not isinstance(t, int) or t >= 2 else 0)
                    dve.scalar_tensor_tensor(out=o_out[v][:], in0=h3[v][:], scalar=rs3[:, 0:1], in1=g_final[:],
                                             op0=ALU.mult, op1=ALU.mult).then_inc(o_done, 1)
                if head:
                    t = s + 1
                    dve.wait_ge(xh_done, t + 1)
                    dve.scalar_tensor_tensor(out=x[:, 1, :], in0=h2[v][:], scalar=rs2[:, 0:1], in1=x[:, 0, :],
                                             op0=ALU.mult, op1=ALU.subtract).then_inc(xl_done, 1)

                def take_x(t):
                    dve.wait_ge(x_mm, t + 1)
                    dve.tensor_copy(pT[v][:], ps_p[:]).then_inc(pT_done, 1)
                    dve.tensor_copy(xT[v][:], ps_x[:]).then_inc(xT_done, 1)

                def residual(h):
                    c = slice(512 * h, 512 * h + 512)
                    dve.wait_ge(th_done, 2 * s + h + 1)
                    dve.wait_ge(up_mm, 2 * s + h + 1)
                    wait(dve, h3_done, 2 * s + h - 1)
                    dve.scalar_tensor_tensor(out=mid[:, h, :], in0=th[:, h, :], scalar=1.0, in1=ps_up[h][:],
                                             op0=ALU.add, op1=ALU.mult).then_inc(mid_done, 1)
                    dve.wait_ge(mid_done, 2 * s + h + 1)
                    dve.scalar_tensor_tensor(out=h3[u][:, c], in0=mid[:, h, :], scalar=0.5, in1=h2[u][:, c],
                                             op0=ALU.mult, op1=ALU.add).then_inc(h3_done, 1)

                if head and not qkv:
                    take_x(s + 1)
                if mid_:
                    if qkv:
                        wait(dve, h3_st[u], done(s - 2, u) if not isinstance(s, int) or s >= 2 else 0)
                    residual(0)
                if mid_:
                    residual(1)
                if head and qkv:
                    take_x(s + 1)
                if mid_:
                    dve.wait_ge(ss3_done, s + 1)
                    wait(dve, rs3_done, s)
                    dve.tensor_scalar(ms3[:], ss3[:], 1.0 / D, EPS, ALU.mult, ALU.add).then_inc(ms3_done, 1)
                if mid_ and qkv:
                    dve.wait_ge(x3h_done, s + 1)
                    dve.scalar_tensor_tensor(out=x3[:, 1, :], in0=h3[u][:], scalar=rs3[:, 0:1], in1=x3[:, 0, :],
                                             op0=ALU.mult, op1=ALU.subtract).then_inc(x3l_done, 1)
                if tail and qkv:
                    t = s - 1
                    at = slice(t, t + 1) if isinstance(t, int) else bass.ds(t, 1)
                    wait(dve, q_st, 32 * t)
                    for h in (0, 1):
                        rotate(t, at, ps_q[h][:], q_out[:, 512 * h:512 * h + 512], 8, h, q_mm, 2 * t + h + 1, True)
                    rotate(t, at, ps_kv[:, 0:KVW], kv_out[:, 0:KVW], NKV, 2, kv_mm, t + 1, False)
                    dve.tensor_copy(kv_out[:, KVW:2 * KVW], ps_kv[:, KVW:2 * KVW]).then_inc(v_done, 1)

            steps(dve, step)

        @block.tensor
        def _(pe):
            def product(dst, lhs, w, kk, c):
                for k in range(kk):
                    mm = mm3(pe, dst, lhs[:, 0, k, :], lhs[:, 1, k, :], w[:, 0, k, c], w[:, 1, k, c], k == 0, k == kk - 1)
                return mm

            def step(s, u, load, head, mid_, tail):
                v = 1 - u
                if tail and qkv:
                    t = s - 1
                    pe.wait_ge(x3l_done, t + 1)
                    if mid_:
                        pe.wait_ge(xT_done, s + 1)
                    for h in (0, 1):
                        for k in range(KD):
                            mm = pe.transpose(ps_x[:, h, k, :], x3[:, h, k * P:(k + 1) * P], C.ident_bf[:])
                    mm.then_inc(x3_mm, 1)

                def gate(h):
                    c = slice(512 * h, 512 * h + 512)
                    if qkv and h == 0:
                        wait(pe, rot_mul, 3 * (s - 2) + 2)
                    wait(pe, th_done, 2 * s + h - 1)
                    product(ps_gate[h][:], xT[u], wg, KD, c).then_inc(gate_mm, 1)

                def up(h):
                    c = slice(512 * h, 512 * h + 512)
                    if qkv and h == 0:
                        wait(pe, rot_mul, 3 * (s - 2) + 3)
                        wait(pe, v_done, s - 1)
                    wait(pe, mid_done, 2 * s + h - 1)
                    product(ps_up[h][:], pT[u], wu, KPLE, c).then_inc(up_mm, 1)

                def turn_head():
                    t = s + 1
                    pe.wait_ge(xl_done, t + 1)
                    pe.wait_ge(pl_done, t + 1)
                    wait(pe, xT_done, t)
                    wait(pe, pT_done, t)
                    if qkv:
                        wait(pe, x3T_done, s if tail else 0)
                    for h in (0, 1):
                        for k in range(KPLE):
                            pe.transpose(ps_p[:, h, k, :], ph[:, h, k * P:(k + 1) * P], C.ident_bf[:])
                    for h in (0, 1):
                        for k in range(KD):
                            mm = pe.transpose(ps_x[:, h, k, :], x[:, h, k * P:(k + 1) * P], C.ident_bf[:])
                    mm.then_inc(x_mm, 1)

                if mid_:
                    pe.wait_ge(xT_done, s + 1)
                    pe.wait_ge(pT_done, s + 1)
                    gate(0)
                    if qkv:
                        up(0)
                    gate(1)
                    if qkv:
                        up(1)
                if head:
                    turn_head()
                if mid_ and not qkv:
                    up(0)
                    up(1)
                if tail and qkv:
                    t = s - 1
                    pe.wait_ge(x3T_done, t + 1)
                    wait(pe, rot_mul, 3 * (t - 1) + 1)
                    product(ps_q[0][:], x3T, wq, KD, slice(0, 512)).then_inc(q_mm, 1)
                    if mid_:
                        pe.wait_ge(th_done, 2 * s + 1)
                    product(ps_q[1][:], x3T, wq, KD, slice(512, 1024)).then_inc(q_mm, 1)
                    if mid_:
                        pe.wait_ge(mid_done, 2 * s + 1)
                    product(ps_kv[:], x3T, wkv, KD, slice(0, 512)).then_inc(kv_mm, 1)

            steps(pe, step)


def attention_phase(nc, A, C):
    NP = NQ // 2
    HALF = NP // 2
    with ExitStack() as stack:
        m = Mem(nc, "att", stack)
        wo = m.sb("wo", [P, 2, KD, D], BF16)
        src = A["w_o"][0].rearrange("(jj s i e) n -> jj i s e n", jj=2, s=2, i=4)
        jobs = [([(slice(0, HEAD), src[c // 4, c % 4, 0]), (slice(HEAD, P), src[c // 4, c % 4, 1])], None,
                 wo[:, 0, c, :], wo[:, 1, c, :]) for c in range(NP)]
        split_weights(nc, C, "aw", [], jobs)

        g_ffn = m.sb("g_ffn", [P, D])
        w_router = m.sb("w_router", [P, KD, NLOG])
        bias = m.sb("bias", [P, NLOG])
        sink = m.sb("sink", [P, NQ])
        q_in = [m.sb(f"q_in{u}", [P, D]) for u in (0, 1)]
        kv_in = [m.sb(f"kv_in{u}", [P, 2 * KVW]) for u in (0, 1)]
        h3 = [m.sb(f"h3_{u}", [P, D]) for u in (0, 1)]
        qT = m.sb("qT", [P, NP, P])
        kT = [m.sb(f"kT{u}", [P, 2, 2, P]) for u in (0, 1)]
        vp = [m.sb(f"v{u}", [P, 2, NKV, P], BF16) for u in (0, 1)]
        W = 2 * P
        score = [m.sb(f"score{c}", [P, 2, W + 1]) for c in range(NP)]
        ER = 4
        ex = [m.sb(f"ex{i}", [P, 2, W + 1]) for i in range(ER)]
        pr = [m.sb(f"pr{i}", [P, 2, 2, W], BF16) for i in (0, 1)]
        prT = [m.sb(f"prT{jj}", [P, 8, HALF, P], BF16) for jj in (0, 1)]
        mx, nmx, esum, rden = (m.sb(n, [P, NQ]) for n in ("mx", "nmx", "esum", "rden"))
        oT = m.sb("oT", [P, 2, KD, P], BF16)
        h4 = [m.sb(f"h4_{u}", [P, D]) for u in (0, 1)]
        hn = m.sb("hn", [P, D])
        hnT = m.sb("hnT", [P, KD, P])
        hrow = [m.sb(f"hrow{u}", [P, 2 * D], BF16) for u in (0, 1)]
        junk = m.sb("junk", [P, D])
        ss, ms, rs = (m.sb(n, [P, 1]) for n in ("ss", "ms", "rs"))
        ps_s = m.ps("s", [P, 2, 2, W])
        ps_p = m.ps("p", [P, 2, 8, P], BF16)
        ps_o = m.ps("o", [P, 2, 512])
        ps_x = m.ps("x", [P, D])
        ps_log, ps_k = ps_o[:, 0, 0:NLOG], ps_o[:, 1, 0:2 * P].rearrange("p (j n) -> p j n", j=2)
        loaded, fixed = m.sems("loaded fixed")
        q_ld, kv_ld, h3_ld, h4_st, row_st = ([m.sem(f"{n}{u}") for u in (0, 1)] for n in ("q_ld", "kv_ld", "h3_ld", "h4_st", "row_st"))
        turn_mm, qT_done, kT_done, vh_done, v_done = m.sems("turn_mm qT_done kT_done vh_done v_done")
        s_mm, top_open, mx_done, nmx_done, e_done, rden_done, ph_done, pl_done, pT_mm, pT_done = m.sems(
            "s_mm top_open mx_done nmx_done e_done rden_done ph_done pl_done pT_mm pT_done")
        pv_mm, oh_done, ol_done, wo_mm, h4_done = m.sems("pv_mm oh_done ol_done wo_mm h4_done")
        ss_done, ms_done, rs_done, hn_done, hi_done, lo_done, hnT_mm, hnT_done, log_mm, log_done = m.sems(
            "ss_done ms_done rs_done hn_done hi_done lo_done hnT_mm hnT_done log_mm log_done")
        q_t = C.q_rows.rearrange("(t p) d -> t p d", p=P)
        kv_t = C.kv_rows.rearrange("(t p) d -> t p d", p=P)
        h3_t = C.h_out.rearrange("(t p) d -> t p d", p=P)
        h4_t = C.h_mid.rearrange("(t p) d -> t p d", p=P)
        row_t = C.hn_rows.rearrange("(t p) d -> t p d", p=P)
        block = stack.enter_context(nc.Block())

        def steps(eng, step):
            step(-1, 1, True, True, False, False, False)
            step(0, 0, True, True, True, False, False)
            step(1, 1, True, True, True, True, False)
            with eng.Fori(1, NT // 2 - 1) as i:
                step(2 * i, 0, True, True, True, True, True)
                step(2 * i + 1, 1, True, True, True, True, True)
            step(NT - 2, 0, False, True, True, True, True)
            step(NT - 1, 1, False, False, True, True, True)
            step(NT, 0, False, False, False, True, True)
            step(NT + 1, 1, False, False, False, False, True)

        def pairs(t, c):
            return NP * t + c + 1

        @block.sync
        def _(sp):
            with nc.allow_non_contiguous_dma(reason="sinks in head-pair order, once"):
                for jj in (0, 1):
                    for k in (0, 1):
                        sp.dma_start(sink[:, 8 * jj + k:8 * jj + 8:2],
                                     row(A["sinks"][0][8 * jj + 4 * k:8 * jj + 4 * k + 4])).then_inc(loaded, 16)
            sp.dma_start(q_in[0][:], q_t[0]).then_inc(q_ld[0], 16)
            sp.dma_start(kv_in[0][:], kv_t[0]).then_inc(kv_ld[0], 16)
            sp.dma_start(g_ffn[:], row(A["g_ffn"][1])).then_inc(loaded, 16)
            load_router(nc, sp, A, w_router, bias, 1, loaded)

            def step(s, u, load, nxt, cur, prev, prev2):
                v = 1 - u
                if load:
                    wait(sp, turn_mm, s + 1)
                    sp.dma_start(q_in[u][:], q_t[s + 2]).then_inc(q_ld[u], 16)
                if cur:
                    wait(sp, h4_done, 2 * (s - 1))
                    sp.dma_start(h3[u][:], h3_t[s]).then_inc(h3_ld[u], 16)
                if prev2:
                    sp.wait_ge(lo_done, s - 1)
                    sp.dma_start(row_t[s - 2], hrow[u][:]).then_inc(row_st[u], 16)
                if load:
                    wait(sp, v_done, s + 1)
                    sp.dma_start(kv_in[u][:], kv_t[s + 2]).then_inc(kv_ld[u], 16)
                if prev:
                    sp.wait_ge(h4_done, 2 * s)
                    sp.dma_start(h4_t[s - 1], h4[v][:]).then_inc(h4_st[v], 16)

            steps(sp, step)
            for u in (0, 1):
                sp.wait_ge(h4_st[u], 8 * NT)
                sp.wait_ge(row_st[u], 8 * NT)

        @block.gpsimd
        def _(pool):
            for u in (0, 1):
                pool.memset(kT[u][:], 0.0).then_inc(fixed, 1)
                pool.memset(vp[u][:], 0.0).then_inc(fixed, 1)

            def heads(t, c):
                pool.wait_ge(rden_done, pairs(t, c))
                wait(pool, pT_mm, pairs(t, c - 2))
                pool.tensor_tensor(pr[c % 2][:, 0, :, :], ex[c % ER][:, :, 0:W],
                                   rden[:, 2 * c:2 * c + 2].unsqueeze(2).to_broadcast([P, 2, W]), ALU.mult).then_inc(ph_done, 1)

            def step(s, u, load, nxt, cur, prev, prev2):
                for c in range(NP):
                    if c == 7 and prev:
                        pool.wait_ge(ms_done, s)
                        wait(pool, hn_done, s - 1)
                        pool.tensor_tensor(rs[:], ms[:], C.minus_half[:], ALU.pow).then_inc(rs_done, 1)
                    if c < NP - 1 and cur:
                        heads(s, c + 1)
                    if c == NP - 1 and nxt:
                        heads(s + 1, 0)

            steps(pool, step)

        @block.scalar
        def _(act):
            def exps(t, c):
                act.wait_ge(nmx_done, pairs(t, c))
                wait(act, pl_done, pairs(t, c - ER))
                for k in (0, 1):
                    n = 2 * c + k
                    e = act.activation(ex[c % ER][:, k, :], score[c][:, k, :], ACT.Exp, bias=nmx[:, n:n + 1],
                                       accum_out=esum[:, n:n + 1])
                e.then_inc(e_done, 1)

            def out_hi(t, jj):
                act.wait_ge(pv_mm, 2 * t + jj + 1)
                wait(act, wo_mm, 2 * t)
                act.activation(oT[:, 0, HALF * jj:HALF * jj + HALF, :], ps_o[:, jj, :].rearrange("p (i n) -> p i n", i=HALF),
                               ACT.Copy).then_inc(oh_done, 1)

            def step(s, u, load, nxt, cur, prev, prev2):
                v = 1 - u
                for c in range(NP):
                    if c == 0 and prev2:
                        act.wait_ge(hn_done, s - 1)
                        wait(act, row_st[u], done(s - 4, u) if not isinstance(s, int) or s >= 4 else 0)
                        act.activation(hrow[u][:, 0:D], hn[:], ACT.Copy).then_inc(hi_done, 1)
                    if c == 1 and prev2:
                        act.wait_ge(hnT_mm, s - 1)
                        wait(act, log_mm, s - 2)
                        act.activation(hnT[:], ps_x[:], ACT.Copy).then_inc(hnT_done, 1)
                    if c == 1 and prev:
                        out_hi(s - 1, 1)
                    if c == 1 and cur:
                        act.wait_ge(kv_ld[u], done(s, u))
                        wait(act, pv_mm, 2 * s)
                        act.wait_ge(fixed, 4)
                        vin = kv_in[u][:, KVW:2 * KVW].rearrange("p (j k e) -> p j k e", k=2, e=HEAD)
                        for k in (0, 1):
                            last = act.activation(vp[u][:, 0, k:NKV:2, k * HEAD:k * HEAD + HEAD], vin[:, :, k, :], ACT.Copy)
                        last.then_inc(vh_done, 1)
                    if c == 6 and prev:
                        act.wait_ge(h4_done, 2 * s)
                        wait(act, ss_done, s - 1)
                        act.activation(junk[:], h4[v][:], ACT.Square, accum_out=ss[:]).then_inc(ss_done, 1)
                    if c == 6 and nxt:
                        act.wait_ge(turn_mm, s + 2)
                        wait(act, s_mm, NP * (s + 1))
                        act.activation(qT[:], ps_x[:], ACT.Copy).then_inc(qT_done, 1)
                    if c == 7 and cur:
                        out_hi(s, 0)
                    if c < NP - 2 and cur:
                        exps(s, c + 2)
                    if c >= NP - 2 and nxt:
                        exps(s + 1, c + 2 - NP)

            steps(act, step)

        @block.vector
        def _(dve):
            dve.wait_ge(loaded, 16 * 9)
            for c in range(NP):
                dve.tensor_copy(score[c][:, :, W:W + 1], sink[:, 2 * c:2 * c + 2].unsqueeze(2)).then_inc(top_open, 1)

            def top(t, c):
                dve.wait_ge(s_mm, pairs(t, c))
                wait(dve, e_done, pairs(t - 1, c))
                dve.sem_inc(top_open, 1)
                mask = C.mask_first if isinstance(t, int) and t == 0 else C.mask
                for k in (0, 1):
                    n = 2 * c + k
                    last = dve.tensor_tensor_reduce(out=score[c][:, k, 0:W], in0=ps_s[:, c % 2, k, :], in1=mask[:],
                                                    scale=1.0, scalar=sink[:, n:n + 1], op0=ALU.add, op1=ALU.max,
                                                    accum_out=mx[:, n:n + 1])
                last.then_inc(mx_done, 1)
                dve.wait_ge(mx_done, pairs(t, c))
                dve.tensor_scalar(nmx[:, 2 * c:2 * c + 2], mx[:, 2 * c:2 * c + 2], -1.0, None, ALU.mult).then_inc(nmx_done, 1)

            def over(t, c):
                dve.wait_ge(e_done, pairs(t, c))
                dve.reciprocal(rden[:, 2 * c:2 * c + 2], esum[:, 2 * c:2 * c + 2]).then_inc(rden_done, 1)

            def rests(t, c):
                dve.wait_ge(ph_done, pairs(t, c))
                for k in (0, 1):
                    n = 2 * c + k
                    last = dve.scalar_tensor_tensor(out=pr[c % 2][:, 1, k, :], in0=ex[c % ER][:, k, 0:W], scalar=rden[:, n:n + 1],
                                                    in1=pr[c % 2][:, 0, k, :], op0=ALU.mult, op1=ALU.subtract)
                last.then_inc(pl_done, 1)

            def turned(t, c):
                jj, i = divmod(c, HALF)
                dve.wait_ge(pT_mm, pairs(t, c))
                if i == 0:
                    wait(dve, pv_mm, 2 * (t - 1) + jj + 1)
                dve.tensor_copy(prT[jj][:, :, i, :], ps_p[:, c % 2, :, :]).then_inc(pT_done, 1)

            def out_lo(t, jj):
                dve.wait_ge(oh_done, 2 * t + jj + 1)
                h = slice(HALF * jj, HALF * jj + HALF)
                dve.tensor_tensor(oT[:, 1, h, :], ps_o[:, jj, :].rearrange("p (i n) -> p i n", i=HALF), oT[:, 0, h, :],
                                  ALU.subtract).then_inc(ol_done, 1)

            def residual(t, par, n):
                c = slice(512 * n, 512 * n + 512)
                dve.wait_ge(wo_mm, 2 * t + n + 1)
                dve.wait_ge(h3_ld[par], done(t, par))
                if n == 0:
                    wait(dve, h4_st[par], done(t - 2, par) if not isinstance(t, int) or t >= 2 else 0)
                dve.tensor_tensor(h4[par][:, c], ps_x[:, c], h3[par][:, c], ALU.add).then_inc(h4_done, 1)

            def step(s, u, load, nxt, cur, prev, prev2):
                v = 1 - u
                for c in range(NP):
                    if c > 0 and cur:
                        turned(s, c - 1)
                    if c == 1 and prev:
                        out_lo(s - 1, 1)
                    if cur:
                        rests(s, c)
                    if c < NP - 1 and cur:
                        over(s, c + 1)
                    if c == 2 and cur:
                        dve.wait_ge(vh_done, s + 1)
                        vin = kv_in[u][:, KVW:2 * KVW].rearrange("p (j k e) -> p j k e", k=2, e=HEAD)
                        for k in (0, 1):
                            at = (slice(k, NKV, 2), slice(k * HEAD, k * HEAD + HEAD))
                            last = dve.tensor_tensor(vp[u][:, 1, at[0], at[1]], vin[:, :, k, :], vp[u][:, 0, at[0], at[1]],
                                                     ALU.subtract)
                        last.then_inc(v_done, 1)
                    if c in (4, 5) and prev:
                        residual(s - 1, v, c - 4)
                    if c == 6 and prev2:
                        dve.wait_ge(log_mm, s - 1)
                        at = slice(s - 2, s - 1) if isinstance(s, int) else bass.ds(s - 2, 1)
                        dve.tensor_tensor(C.logits[:, at, :].rearrange("p a b -> p (a b)"), ps_log, bias[:],
                                          ALU.add).then_inc(log_done, 1)
                    if c == 6 and nxt:
                        dve.wait_ge(turn_mm, s + 2)
                        wait(dve, s_mm, NP * (s + 1))
                        dve.wait_ge(fixed, 4)
                        for k in (0, 1):
                            rows = slice(HEAD * k, HEAD * k + HEAD)
                            last = dve.tensor_copy(kT[v][rows, :, k, :], ps_k[rows, :, :])
                        last.then_inc(kT_done, 1)
                    if c == 6 and prev:
                        dve.wait_ge(ss_done, s)
                        dve.tensor_scalar(ms[:], ss[:], 1.0 / D, EPS, ALU.mult, ALU.add).then_inc(ms_done, 1)
                    if c < NP - 2 and cur:
                        top(s, c + 2)
                    if c == 7 and nxt:
                        top(s + 1, 0)
                    if c == 7 and cur:
                        turned(s, 7)
                    if c == 7 and nxt:
                        top(s + 1, 1)
                        over(s + 1, 0)
                    if c == 0 and prev2:
                        dve.wait_ge(hi_done, s - 1)
                        dve.wait_ge(hn_done, s - 1)
                        dve.tensor_tensor(hrow[u][:, D:2 * D], hn[:], hrow[u][:, 0:D], ALU.subtract).then_inc(lo_done, 1)
                    if c == 7 and cur:
                        out_lo(s, 0)
                    if c == 7 and prev:
                        dve.wait_ge(rs_done, s)
                        wait(dve, hnT_mm, s - 1)
                        dve.scalar_tensor_tensor(out=hn[:], in0=h4[v][:], scalar=rs[:, 0:1], in1=g_ffn[:],
                                                 op0=ALU.mult, op1=ALU.mult).then_inc(hn_done, 1)

            steps(dve, step)

        @block.tensor
        def _(pe):
            pe.wait_ge(loaded, 16 * 9)

            def scores(t, par, c):
                if c < 2:
                    pe.wait_ge(qT_done, t + 1)
                    pe.wait_ge(kT_done, t + 1)
                wait(pe, mx_done, pairs(t, c - 2))
                jj = c // HALF
                for b, keys in ((0, kT[1 - par]), (1, kT[par])):
                    mm = pe.matmul(ps_s[:, c % 2, :, b * P:(b + 1) * P], qT[:, c, :], keys[:, jj, :, :],
                                   start=True, stop=True)
                mm.then_inc(s_mm, 1)

            def turn(t, c):
                pe.wait_ge(pl_done, pairs(t, c))
                wait(pe, pT_done, pairs(t, c - 2))
                for part in (0, 1):
                    for k in (0, 1):
                        for b in (0, 1):
                            mm = pe.transpose(ps_p[:, c % 2, 4 * part + 2 * k + b, :], pr[c % 2][:, part, k, b * P:(b + 1) * P],
                                              C.ident_bf[:])
                mm.then_inc(pT_mm, 1)

            def weigh(t, par, jj):
                pe.wait_ge(pT_done, pairs(t, HALF * jj + HALF - 1))
                pe.wait_ge(v_done, t + 1)
                wait(pe, ol_done, 2 * (t - 1) + jj + 1)
                out = ps_o[:, jj, :].rearrange("p (i n) -> p i n", i=HALF)
                n = 0
                for k in (0, 1):
                    for b, val in ((0, vp[1 - par]), (1, vp[par])):
                        hi, lo = (prT[jj][:, 4 * part + 2 * k + b, :, :] for part in (0, 1))
                        v_hi, v_lo = (val[:, part, 2 * jj + k, :] for part in (0, 1))
                        mm = mm3(pe, out, v_hi, v_lo, hi, lo, n == 0, n == 3)
                        n += 1
                mm.then_inc(pv_mm, 1)

            def project(n, jj):
                c = slice(512 * n, 512 * n + 512)
                for k in range(HALF * jj, HALF * jj + HALF):
                    mm = mm3(pe, ps_x[:, c], oT[:, 0, k, :], oT[:, 1, k, :], wo[:, 0, k, c], wo[:, 1, k, c],
                             k == 0, k == KD - 1)
                return mm

            def step(s, u, load, nxt, cur, prev, prev2):
                v = 1 - u
                for c in range(NP):
                    if c == 6 and nxt:
                        t = s + 1
                        pe.wait_ge(q_ld[v], done(t, v))
                        pe.wait_ge(kv_ld[v], done(t, v))
                        wait(pe, h4_done, 2 * s)
                        wait(pe, ol_done, 2 * s)
                        for k in range(KD):
                            pe.transpose(ps_x[:, k * P:(k + 1) * P], q_in[v][:, k * P:(k + 1) * P], C.ident[:])
                        for j in (0, 1):
                            mm = pe.transpose(ps_k[:, j, :], kv_in[v][:, j * P:(j + 1) * P], C.ident[:])
                        mm.then_inc(turn_mm, 1)
                    if c < NP - 2 and cur:
                        scores(s, u, c + 2)
                    if c == 0 and prev:
                        if cur:
                            pe.wait_ge(kT_done, s + 1)
                        weigh(s - 1, v, 1)
                    if c == 0 and prev2:
                        pe.wait_ge(hn_done, s - 1)
                        if cur:
                            pe.wait_ge(qT_done, s + 1)
                        for k in range(KD):
                            mm = pe.transpose(ps_x[:, k * P:(k + 1) * P], hn[:, k * P:(k + 1) * P], C.ident[:])
                        mm.then_inc(hnT_mm, 1)
                    if c == 1 and prev:
                        if prev2:
                            pe.wait_ge(hnT_done, s - 1)
                        if cur:
                            pe.wait_ge(qT_done, s + 1)
                        pe.wait_ge(ol_done, 2 * s - 1)
                        project(0, 0)
                    if c == 2 and prev:
                        project(1, 0)
                    if c in (3, 4) and prev:
                        pe.wait_ge(ol_done, 2 * s)
                        project(c - 3, 1).then_inc(wo_mm, 1)
                    if c == 5 and prev2:
                        pe.wait_ge(hnT_done, s - 1)
                        if prev:
                            pe.wait_ge(ol_done, 2 * s - 1)
                        for k in range(KD):
                            mm = pe.matmul(ps_log, hnT[:, k, :], w_router[:, k, :], start=k == 0, stop=k == KD - 1)
                        mm.then_inc(log_mm, 1)
                    if cur:
                        turn(s, c)
                    if c == 6 and cur:
                        wait(pe, log_done, s - 1)
                        weigh(s, u, 0)
                    if c >= NP - 2 and nxt:
                        scores(s + 1, v, c + 2 - NP)

            steps(pe, step)


class Shared:

    def __init__(self, nc, stack):
        m = Mem(nc, "all", stack)
        self.ident = m.sb("ident", [P, P])
        self.ident_bf = m.sb("ident_bf", [P, P], BF16)
        self.before = m.sb("before", [P, P])
        self.ones = m.sb("ones", [P, P])
        self.iota = m.sb("iota", [P, P])
        self.lane = m.sb("lane", [P, 1])
        self.minus_half = m.sb("minus_half", [P, 1])
        self.zero = m.sb("zero", [P, 1])
        self.band = m.sb("band", [P, len(WINDOWS), P], BF16)
        self.band_first = m.sb("band_first", [P, 2, len(WINDOWS), P], BF16)
        self.band_prev = m.sb("band_prev", [P, len(WINDOWS), TAIL], BF16)
        self.mask = m.sb("mask", [P, 2 * P])
        self.mask_first = m.sb("mask_first", [P, 2 * P])
        self.logits = m.sb("logits", [P, NT, NLOG])
        self.gates = m.sb("gates", [P, 2, NT])
        self.slot_row = m.sb("slot_row", [P, 2, NT], I32)
        self.slot_token = m.sb("slot_token", [P, MAX_TILES + 1], I32)
        self.ends = m.sb("ends", [1, NE + 1], I32)
        dram = lambda name, shape, dt=F32: nc.dram_tensor(name, shape, dt, kind="Internal").ap()
        self.h_mid = dram("h_mid", [T, D])
        self.h_out = dram("h_out", [T, D])
        self.hn_rows = dram("hn_rows", [T, 2 * D], BF16)
        self.y_rows = dram("y_rows", [(MAX_TILES + 1) * P, D])
        self.q_rows = dram("q_rows", [T, D])
        self.kv_rows = dram("kv_rows", [T, 2 * KVW])


def build(nc, A, out, phases=None):
    with ExitStack() as stack:
        C = Shared(nc, stack)
        todo = [lambda: constants_phase(nc, C), lambda: pool_phase(nc, A, C), lambda: route_phase(nc, C, 0),
                lambda: experts_phase(nc, A, C, 0), lambda: combine_phase(nc, A, C, 0, out),
                lambda: attention_phase(nc, A, C), lambda: route_phase(nc, C, 1),
                lambda: experts_phase(nc, A, C, 1), lambda: combine_phase(nc, A, C, 1, out)]
        for n, phase in enumerate(todo):
            if phases is None or n in phases:
                phase()


_INS = ['x', 'p', 'positions', 'g_mix', 'g_ffn', 'pool_w', 'pool_scale', 'g_kv', 'w_k', 'w_v', 'w_q', 'w_o', 'sinks',
        'w_group_router', 'b_group_router', 'w_expert_router', 'b_expert_router',
        'w_exp_gate', 'w_exp_up', 'w_exp_down', 'g_ple', 'w_ple_gate', 'w_ple_up', 'g_final']


def kernel(**inputs):
    import concourse.bacc as bacc
    from concourse.bass_utils import run_bass_kernel_spmd

    nc = bacc.Bacc("TRN2", target_bir_lowering=False, num_devices=1)
    arrays, A = {}, {}
    for name in _INS:
        arrays[f"in_{name}"] = a = np.ascontiguousarray(inputs[name])
        A[name] = nc.dram_tensor(f"in_{name}", a.shape, mybir.dt.from_np(a.dtype), kind="ExternalInput").ap()
    out = nc.dram_tensor("out", [1, T, D], F32, kind="ExternalOutput").ap()
    build(nc, A, out)
    r = run_bass_kernel_spmd(nc, [arrays], core_ids=[0])
    return r.results[0]["out"]
```
